# Optimizing a Trainium2 kernel written in Bass

```python
import math
import jax, jax.numpy as jnp
from jax import lax
import numpy as np

D_MODEL = 2048
BATCH = 1
SEQ = 256
DEPTH = 1
DEC_BATCH = 8
DEC_SEQ = 4
PAST_LEN = 1024
PAGE_SIZE = 128

MIX_WIDTH = D_MODEL
A_WIDTH = MIX_WIDTH // 2
A_GROUPS = 8
A_CH = A_WIDTH // A_GROUPS
A_CHUNK = 128
B_WIDTH = MIX_WIDTH - A_WIDTH
B_HEADS = 8
B_HEAD_DIM = B_WIDTH // B_HEADS
B_KV_HEADS = 2
B_GQA = B_HEADS // B_KV_HEADS
IDX_HEADS = 16
IDX_DIM = 64
TOPK_MAX = 256
Q_BLOCK = 128
REL_BUCKETS = 32
REL_MAX_DIST = 128
MEM_LEN = 256
MEM_HEADS = 4
MEM_HEAD_DIM = 128
MEM_WIDTH = MEM_HEADS * MEM_HEAD_DIM
N_GROUPS = 4
EXPERTS_PER_GROUP = 4
N_EXPERTS = N_GROUPS * EXPERTS_PER_GROUP
TOP_K_IN_GROUP = 2
EXPERT_FF = 512
EPS = 1e-6
IN_SIZES = (A_WIDTH, A_WIDTH, B_HEADS * B_HEAD_DIM, B_KV_HEADS * B_HEAD_DIM, B_KV_HEADS * B_HEAD_DIM, IDX_HEADS * IDX_DIM, IDX_DIM, IDX_HEADS)
IN_COLS = 2 * A_WIDTH + B_HEADS * B_HEAD_DIM + 2 * B_KV_HEADS * B_HEAD_DIM + IDX_HEADS * IDX_DIM + IDX_DIM + IDX_HEADS

kernel_name = 'hymba_gmlp_dsa_hmoe_decode_step'

def rms_norm(x, gain):
    xf = x.astype(jnp.float32)
    y = xf * lax.rsqrt(jnp.mean(xf * xf, axis=-1, keepdims=True) + EPS)
    return (y * gain.astype(jnp.float32)).astype(x.dtype)

def t5_bucket(dist):
    max_exact = REL_BUCKETS // 2
    d = jnp.maximum(dist, 0)
    ratio = jnp.log(jnp.maximum(d, 1).astype(jnp.float32) / max_exact) / math.log(REL_MAX_DIST / max_exact)
    large = jnp.minimum(max_exact + (ratio * (REL_BUCKETS - max_exact)).astype(jnp.int32), REL_BUCKETS - 1)
    return jnp.where(d < max_exact, d, large)

def gather_rows(rows, idx):
    return jax.vmap(lambda r, i: r[i])(rows, idx)

def project_mixer(n, w_in, a_vnorm, b_qnorm, b_knorm):
    B, T, _ = n.shape
    p = jnp.einsum('btd,dc->btc', n, w_in)
    offs = [int(o) for o in np.cumsum(IN_SIZES)[:-1]]
    a_u, a_v, b_q, b_k, b_v, i_q, i_k, i_w = jnp.split(p, offs, axis=-1)
    u = jax.nn.gelu(a_u, approximate=False)
    vn = rms_norm(jax.nn.gelu(a_v, approximate=False).reshape(B, T, A_GROUPS, A_CH), a_vnorm)
    q = rms_norm(b_q.reshape(B, T, B_HEADS, B_HEAD_DIM), b_qnorm)
    k = rms_norm(b_k.reshape(B, T, B_KV_HEADS, B_HEAD_DIM), b_knorm)
    v = b_v.reshape(B, T, B_KV_HEADS, B_HEAD_DIM)
    qi = i_q.reshape(B, T, IDX_HEADS, IDX_DIM)
    wi = i_w * (IDX_HEADS ** -0.5)
    return u, vn, q, k, v, qi, wi, i_k

def spatial_mix(vc, a_ws, a_b):
    P = vc.shape[2]
    ws = a_ws[:, :P, :P] * jnp.tril(jnp.ones((P, P), a_ws.dtype))
    return jnp.einsum('gts,bnsgc->bntgc', ws, vc) + a_b[:, :P].T[None, None, :, :, None]

def indexer_scores(qi, wi, ki):
    s = jnp.einsum('bqhd,bld->bqhl', qi, ki).astype(jnp.float32) * (IDX_DIM ** -0.5)
    return jnp.einsum('bqh,bqhl->bql', wi.astype(jnp.float32), jax.nn.relu(s))

def sparse_attend(q, k_sel, v_sel, rel_b, valid):
    B, Q, H, Dh = q.shape
    K = k_sel.shape[2]
    qg = q.reshape(B, Q, B_KV_HEADS, B_GQA, Dh)
    logits = jnp.einsum('bqkgd,bqskd->bqkgs', qg, k_sel).astype(jnp.float32) * (Dh ** -0.5)
    logits = logits + rel_b.astype(jnp.float32).reshape(B, Q, K, B_KV_HEADS, B_GQA).transpose(0, 1, 3, 4, 2)
    logits = jnp.where(valid[:, :, None, None, :], logits, -jnp.inf)
    p = jax.nn.softmax(logits, axis=-1).astype(v_sel.dtype)
    o = jnp.einsum('bqkgs,bqskd->bqkgd', p, v_sel)
    return o.reshape(B, Q, H * Dh)

def dsa_prompt(q, k, v, qi, wi, ki, rel_bias):
    B, T = q.shape[:2]
    topk = min(TOPK_MAX, T // 4)
    key_pos = jnp.arange(T)

    def block(i):
        s = i * Q_BLOCK
        qb = lax.dynamic_slice_in_dim(q, s, Q_BLOCK, axis=1)
        qib = lax.dynamic_slice_in_dim(qi, s, Q_BLOCK, axis=1)
        wib = lax.dynamic_slice_in_dim(wi, s, Q_BLOCK, axis=1)
        qpos = s + jnp.arange(Q_BLOCK)
        sc = indexer_scores(qib, wib, ki)
        sc = jnp.where(key_pos[None, None, :] <= qpos[None, :, None], sc, -jnp.inf)
        _, sel = lax.top_k(sc, topk)
        valid = sel <= qpos[None, :, None]
        rel_b = rel_bias[t5_bucket(qpos[None, :, None] - sel)]
        return sparse_attend(qb, gather_rows(k, sel), gather_rows(v, sel), rel_b, valid)

    out = lax.map(block, jnp.arange(T // Q_BLOCK))
    return out.transpose(1, 0, 2, 3).reshape(B, T, B_WIDTH)

def dsa_sample(q, k_new, v_new, qi, wi, ki_new, cache_k, cache_v, cache_idx_k, page_table, rel_bias):
    Bd, S = q.shape[:2]
    past = page_table.shape[1] * PAGE_SIZE
    n_keys = past + S
    topk = min(TOPK_MAX, n_keys // 4)
    ki_past = cache_idx_k[page_table].reshape(Bd, past, IDX_DIM)
    ki_all = jnp.concatenate([ki_past, ki_new.astype(ki_past.dtype)], axis=1)
    qpos = past + jnp.arange(S)
    sc = indexer_scores(qi, wi, ki_all)
    sc = jnp.where(jnp.arange(n_keys)[None, None, :] <= qpos[None, :, None], sc, -jnp.inf)
    _, sel = lax.top_k(sc, topk)
    valid = sel <= qpos[None, :, None]
    sp = jnp.minimum(sel, past - 1)
    phys = gather_rows(page_table, sp // PAGE_SIZE)
    off = sp % PAGE_SIZE
    sn = jnp.clip(sel - past, 0, S - 1)
    is_past = (sel < past)[..., None, None]
    k_sel = jnp.where(is_past, cache_k[phys, off], gather_rows(k_new, sn).astype(cache_k.dtype))
    v_sel = jnp.where(is_past, cache_v[phys, off], gather_rows(v_new, sn).astype(cache_v.dtype))
    rel_b = rel_bias[t5_bucket(qpos[None, :, None] - sel)]
    return sparse_attend(q, k_sel, v_sel, rel_b, valid)

def memory_kv(mem, mem_wk, mem_wv, mem_knorm):
    B, M, _ = mem.shape
    mk = rms_norm(jnp.einsum('bmd,dc->bmc', mem, mem_wk).reshape(B, M, MEM_HEADS, MEM_HEAD_DIM), mem_knorm)
    mv = jnp.einsum('bmd,dc->bmc', mem, mem_wv).reshape(B, M, MEM_HEADS, MEM_HEAD_DIM)
    return mk, mv

def memory_attend(n, mk, mv, mem_wq, mem_qnorm, mem_wo):
    B, T, _ = n.shape
    q = rms_norm(jnp.einsum('btd,dc->btc', n, mem_wq).reshape(B, T, MEM_HEADS, MEM_HEAD_DIM), mem_qnorm)
    logits = jnp.einsum('bthd,bmhd->bhtm', q, mk.astype(q.dtype)).astype(jnp.float32) * (MEM_HEAD_DIM ** -0.5)
    p = jax.nn.softmax(logits, axis=-1).astype(n.dtype)
    o = jnp.einsum('bhtm,bmhd->bthd', p, mv.astype(n.dtype)).reshape(B, T, MEM_WIDTH)
    return jnp.einsum('btc,cd->btd', o, mem_wo)

def hier_moe(n, w_group, b_group, w_router, b_router, w_gate, w_up, w_down):
    B, T, D = n.shape
    xf = n.reshape(B * T, D)
    g_prob = jax.nn.softmax((xf @ w_group + b_group).astype(jnp.float32), axis=-1)
    g_sel = jnp.argmax(g_prob, axis=-1)
    g_gate = jnp.take_along_axis(g_prob, g_sel[:, None], axis=1)
    e_logits = (xf @ w_router + b_router).astype(jnp.float32).reshape(-1, N_GROUPS, EXPERTS_PER_GROUP)
    e_logits = jnp.take_along_axis(e_logits, g_sel[:, None, None], axis=1)[:, 0]
    top_w, top_i = lax.top_k(jax.nn.softmax(e_logits, axis=-1), TOP_K_IN_GROUP)
    top_w = top_w / jnp.sum(top_w, axis=-1, keepdims=True) * g_gate
    expert_id = g_sel[:, None] * EXPERTS_PER_GROUP + top_i
    combine = jnp.einsum('nk,nke->ne', top_w, jax.nn.one_hot(expert_id, N_EXPERTS, dtype=jnp.float32)).astype(xf.dtype)
    y = jnp.zeros_like(xf)
    for e in range(N_EXPERTS):
        h = jax.nn.silu(xf @ w_gate[e]) * (xf @ w_up[e])
        y = y + combine[:, e:e + 1] * (h @ w_down[e])
    return y.reshape(B, T, D)

def post_mixer(h, mix, mk, mv, w_out, norm_mem, mem_wq, mem_qnorm, mem_wo, norm_ffn,
               w_group, b_group, w_router, b_router, w_gate, w_up, w_down):
    h = h + jnp.einsum('btc,cd->btd', mix, w_out)
    h = h + memory_attend(rms_norm(h, norm_mem), mk, mv, mem_wq, mem_qnorm, mem_wo)
    return h + hier_moe(rms_norm(h, norm_ffn), w_group, b_group, w_router, b_router, w_gate, w_up, w_down)

def setup_inputs(seed: int = 0) -> dict:
    key = jax.random.key(seed)
    ks = jax.random.split(key, 40)

    def nrm(i, shape, scale):
        return jax.random.normal(ks[i], shape, jnp.float32) * scale

    def gain(i, shape):
        return 1.0 + nrm(i, shape, 0.02)

    L = DEPTH
    n_pages = PAST_LEN // PAGE_SIZE
    n_pool = (DEC_BATCH * n_pages * 5 + 3) // 4
    perm = jax.random.permutation(ks[0], n_pool)
    page_table = perm[:DEC_BATCH * n_pages].reshape(DEC_BATCH, n_pages).astype(jnp.int32)
    return {
        'x_prompt': nrm(1, (BATCH, SEQ, D_MODEL), 1.0),
        'x_sample': nrm(2, (DEC_BATCH, DEC_SEQ, D_MODEL), 1.0),
        'cache_k': nrm(3, (L, n_pool, PAGE_SIZE, B_KV_HEADS, B_HEAD_DIM), 1.0),
        'cache_v': nrm(4, (L, n_pool, PAGE_SIZE, B_KV_HEADS, B_HEAD_DIM), 1.0),
        'cache_idx_k': nrm(5, (L, n_pool, PAGE_SIZE, IDX_DIM), 1.0),
        'cache_mem_k': nrm(6, (L, DEC_BATCH, MEM_LEN, MEM_HEADS, MEM_HEAD_DIM), 1.0),
        'cache_mem_v': nrm(7, (L, DEC_BATCH, MEM_LEN, MEM_HEADS, MEM_HEAD_DIM), 1.0),
        'page_table': page_table,
        'mem_prompt': nrm(8, (BATCH, MEM_LEN, D_MODEL), 1.0),
        'norm_mix': gain(9, (L, D_MODEL)),
        'w_in': nrm(10, (L, D_MODEL, IN_COLS), D_MODEL ** -0.5),
        'a_vnorm': gain(11, (L, A_GROUPS, A_CH)),
        'a_ws': nrm(12, (L, A_GROUPS, A_CHUNK, A_CHUNK), A_CHUNK ** -0.5),
        'a_b': gain(13, (L, A_GROUPS, A_CHUNK)),
        'b_qnorm': gain(14, (L, B_HEAD_DIM)),
        'b_knorm': gain(15, (L, B_HEAD_DIM)),
        'rel_bias': nrm(16, (REL_BUCKETS, B_HEADS), 0.5),
        'w_out': nrm(17, (L, MIX_WIDTH, D_MODEL), MIX_WIDTH ** -0.5),
        'norm_mem': gain(18, (L, D_MODEL)),
        'mem_wq': nrm(19, (L, D_MODEL, MEM_WIDTH), D_MODEL ** -0.5),
        'mem_wk': nrm(20, (L, D_MODEL, MEM_WIDTH), D_MODEL ** -0.5),
        'mem_wv': nrm(21, (L, D_MODEL, MEM_WIDTH), D_MODEL ** -0.5),
        'mem_qnorm': gain(22, (L, MEM_HEAD_DIM)),
        'mem_knorm': gain(23, (L, MEM_HEAD_DIM)),
        'mem_wo': nrm(24, (L, MEM_WIDTH, D_MODEL), MEM_WIDTH ** -0.5),
        'norm_ffn': gain(25, (L, D_MODEL)),
        'w_group': nrm(26, (L, D_MODEL, N_GROUPS), D_MODEL ** -0.5),
        'b_group': nrm(27, (L, N_GROUPS), 0.01),
        'w_router': nrm(28, (L, D_MODEL, N_EXPERTS), D_MODEL ** -0.5),
        'b_router': nrm(29, (L, N_EXPERTS), 0.01),
        'w_gate': nrm(30, (L, N_EXPERTS, D_MODEL, EXPERT_FF), D_MODEL ** -0.5),
        'w_up': nrm(31, (L, N_EXPERTS, D_MODEL, EXPERT_FF), D_MODEL ** -0.5),
        'w_down': nrm(32, (L, N_EXPERTS, EXPERT_FF, D_MODEL), EXPERT_FF ** -0.5),
    }

def reference(x_prompt, x_sample, cache_k, cache_v, cache_idx_k, cache_mem_k, cache_mem_v, page_table,
              mem_prompt, norm_mix, w_in, a_vnorm, a_ws, a_b, b_qnorm, b_knorm, rel_bias, w_out,
              norm_mem, mem_wq, mem_wk, mem_wv, mem_qnorm, mem_knorm, mem_wo, norm_ffn,
              w_group, b_group, w_router, b_router, w_gate, w_up, w_down):
    hp, hs = x_prompt, x_sample
    Bp, T, _ = x_prompt.shape
    Bd, S, _ = x_sample.shape
    k_p, v_p, ki_p, mk_p, mv_p, k_s, v_s, ki_s, cv_s = [], [], [], [], [], [], [], [], []
    for l in range(DEPTH):
        ffn_args = (w_out[l], norm_mem[l], mem_wq[l], mem_qnorm[l], mem_wo[l], norm_ffn[l],
                    w_group[l], b_group[l], w_router[l], b_router[l], w_gate[l], w_up[l], w_down[l])
        u, vn, q, k, v, qi, wi, ki = project_mixer(rms_norm(hp, norm_mix[l]), w_in[l], a_vnorm[l], b_qnorm[l], b_knorm[l])
        a_out = u * spatial_mix(vn.reshape(Bp, T // A_CHUNK, A_CHUNK, A_GROUPS, A_CH), a_ws[l], a_b[l]).reshape(Bp, T, A_WIDTH)
        b_out = dsa_prompt(q, k, v, qi, wi, ki, rel_bias)
        mk, mv = memory_kv(mem_prompt, mem_wk[l], mem_wv[l], mem_knorm[l])
        hp = post_mixer(hp, jnp.concatenate([a_out, b_out], axis=-1), mk, mv, *ffn_args)
        k_p.append(k); v_p.append(v); ki_p.append(ki); mk_p.append(mk); mv_p.append(mv)
        u, vn, q, k, v, qi, wi, ki = project_mixer(rms_norm(hs, norm_mix[l]), w_in[l], a_vnorm[l], b_qnorm[l], b_knorm[l])
        a_out = u * spatial_mix(vn[:, None], a_ws[l], a_b[l]).reshape(Bd, S, A_WIDTH)
        b_out = dsa_sample(q, k, v, qi, wi, ki, cache_k[l], cache_v[l], cache_idx_k[l], page_table, rel_bias)
        hs = post_mixer(hs, jnp.concatenate([a_out, b_out], axis=-1), cache_mem_k[l], cache_mem_v[l], *ffn_args)
        k_s.append(k); v_s.append(v); ki_s.append(ki); cv_s.append(vn)
    new_k_prompt = jnp.stack(k_p)
    new_v_prompt = jnp.stack(v_p)
    new_idx_k_prompt = jnp.stack(ki_p)
    new_mem_k_prompt = jnp.stack(mk_p)
    new_mem_v_prompt = jnp.stack(mv_p)
    new_k_sample = jnp.stack(k_s)
    new_v_sample = jnp.stack(v_s)
    new_idx_k_sample = jnp.stack(ki_s)
    new_chunk_v_sample = jnp.stack(cv_s)
    return (hp, hs, new_k_prompt, new_v_prompt, new_idx_k_prompt, new_mem_k_prompt, new_mem_v_prompt,
            new_k_sample, new_v_sample, new_idx_k_sample, new_chunk_v_sample)


_drawn_inputs = setup_inputs


def setup_inputs(seed=0):
    import zlib

    import numpy as np

    out = dict(_drawn_inputs(seed))
    spreads = {}
    factors = {'a_vnorm': 7.997,
     'a_b': 3.635,
     'b_qnorm': 8.0,
     'b_knorm': 2.815,
     'norm_mem': 21.775,
     'mem_qnorm': 22.837,
     'b_group': 25.898,
     'b_router': 32.635,
     'norm_ffn': 2.915}
    for name, (base, spread) in spreads.items():
        noise = np.random.default_rng([zlib.crc32(name.encode()), seed]).standard_normal(out[name].shape)
        drawn = base * np.exp(spread * noise) if base else spread * noise
        out[name] = __import__('jax').numpy.asarray(drawn.astype(out[name].dtype))
    for name, factor in factors.items():
        out[name] = (out[name] * factor).astype(out[name].dtype)
    return out
```

```python
import numpy as np
import concourse.bass as bass
from concourse import mybir
from contextlib import ExitStack

F32 = mybir.dt.float32
I32 = mybir.dt.int32
U32 = mybir.dt.uint32
ALU = mybir.AluOpType
ACT = mybir.ActivationFunctionType
AX = mybir.AxisListType

D = 2048
T = 256
NB, NS = 8, 4
R = NB * NS
NT = T + R
KT = D // 128
EPS = 1e-6
PAST, PAGE = 1024, 128
NPAGE = PAST // PAGE
NKEY = PAST + NS
TOPK_P = 64
TOPK_S = 256
NEXP, FF = 16, 512
CAP = 64
NOVF = 8
NBLK = NEXP + NOVF
BIG = 1.0e30
TAKEN = -3.0e38
SCALE = 128.0 ** -0.5
ROWS = (128, 128, R)
CHUNKS = (9, 7, 8, 6, 4, 5, 2, 3, 0, 1)
TOPK_STEP = 6

CONST_COLS, _at = {}, 0
for _name, _w in (("ident", 128), ("tril", 128), ("rank", 128), ("ones", 128), ("causal", 128),
                  ("blk", 128), ("pick", 256), ("wmask", 256), ("newmask", 64), ("newcausal", 4),
                  ("relmask", 32), ("tok", 3), ("sub", 1), ("page", 8), ("iota_e", 16), ("iota_b", 8), ("fold", 32), ("iota_r", 64)):
    CONST_COLS[_name] = (_at, _w)
    _at += _w
NCONST = _at
BUCKET_COLS = NKEY + 384


def t5_bucket(dist):
    d = np.maximum(dist, 0)
    ratio = np.log(np.maximum(d, 1).astype(np.float32) / np.float32(16)) / np.float32(np.log(8.0))
    large = np.minimum(16 + (ratio * np.float32(16)).astype(np.int32), 31)
    return np.where(d < 16, d, large)


def shape_constants():
    c = np.zeros((128, NCONST), np.float32)

    def put(name, a):
        at, w = CONST_COLS[name]
        c[:a.shape[0], at:at + w] = a
    p, f = np.arange(128)[:, None], np.arange(128)[None, :]
    put("ident", (p == f).astype(np.float32))
    put("tril", (f <= p).astype(np.float32))
    put("rank", (p < f).astype(np.float32))
    put("ones", np.ones((128, 128), np.float32))
    put("causal", np.where(f <= p, 0, -BIG).astype(np.float32))
    put("blk", ((p // 4 == f // 4) & (f % 4 <= p % 4)).astype(np.float32))
    r, b, h, q = np.ogrid[0:32, 0:8, 0:8, 0:4]
    put("pick", ((r == b * 4 + q) & (h >= 0)).astype(np.float32).reshape(32, 256))
    r, b, b2, q2 = np.ogrid[0:64, 0:8, 0:8, 0:4]
    put("wmask", ((r % 4 == q2) & (b == b2)).astype(np.float32).reshape(64, 256))
    r, t, k = np.ogrid[0:128, 0:2, 0:32]
    put("newmask", ((t * 4 + r // 32) == k // 4).astype(np.float32).reshape(128, 64))
    r, s = np.ogrid[0:32, 0:4]
    put("newcausal", np.where(s <= r % 4, 0, -BIG).astype(np.float32))
    r, h, q = np.ogrid[0:128, 0:8, 0:4]
    put("relmask", ((r // 32 == q) & (h >= 0)).astype(np.float32).reshape(128, 32))
    put("tok", (p + 128 * np.arange(3)[None, :]).astype(np.float32))
    put("sub", (p % 16).astype(np.float32))
    put("page", (p // 16 == np.arange(8)[None, :]).astype(np.float32))
    put("iota_e", np.broadcast_to(np.arange(16), (128, 16)).astype(np.float32))
    put("iota_b", np.broadcast_to(np.arange(8), (128, 8)).astype(np.float32))
    put("iota_r", np.broadcast_to(np.arange(64), (128, 64)).astype(np.float32))
    put("fold", (p % 32 == np.arange(32)[None, :]).astype(np.float32))
    bk = np.zeros((128, BUCKET_COLS), np.float32)
    for qq in range(4):
        bu = t5_bucket(PAST + qq - np.arange(NKEY))
        bk[qq * 32 + bu, np.arange(NKEY)] = 1
    bu = t5_bucket(255 - np.arange(384))
    bk[bu, NKEY + np.arange(384)] = 1
    return c, bk


def decode_step(nc, consts, buckets, x_prompt, x_sample, cache_k, cache_v, cache_idx_k, cache_mem_k,
                cache_mem_v, page_table, mem_prompt, norm_mix, w_in, a_vnorm, a_ws, a_b, b_qnorm,
                b_knorm, rel_bias, w_out, norm_mem, mem_wq, mem_wk, mem_wv, mem_qnorm, mem_knorm,
                mem_wo, norm_ffn, w_group, b_group, w_router, b_router, w_gate, w_up, w_down,
                y_prompt, y_sample, o_k, o_v, o_ki, o_mk, o_mv, o_ks, o_vs, o_kis, o_cvs):
    ctx = ExitStack()
    with ctx:
        def sb(name, w, dt=F32):
            return ctx.enter_context(nc.sbuf_tensor(name, [128, w], dt))

        def sem(name):
            return ctx.enter_context(nc.semaphore(name))

        def dram(name, shape, dt=F32):
            return nc.dram_tensor(name, shape, dt, kind="Internal").ap()

        SLOT = 2048
        NSLOT = 4
        MSLOT = 4096
        ring = sb("ring", 6 * MSLOT)

        def slot(i):
            return ring[:, (i % NSLOT) * SLOT:(i % NSLOT + 1) * SLOT].rearrange("p (k n) -> p k n", k=4)

        cursor = [NSLOT * SLOT]

        def early(w):
            at = cursor[0]
            cursor[0] += w
            assert cursor[0] <= 6 * MSLOT
            return ring[:, at:at + w]
        stageM = early(4096)
        vn = early(2048).rearrange("p (t c) -> p t c", t=2)
        vnS = early(256).rearrange("p (c d) -> p c d", c=2)
        qT = early(2048).rearrange("p (h t) -> p h t", h=8)
        qiT = early(2048).rearrange("p (h t) -> p h t", h=8)
        kT = early(512).rearrange("p (h t) -> p h t", h=2)
        vP = early(512).rearrange("p (t c) -> p t c", t=2)
        kiT = early(NT)
        QZ, gav, gavS, Wz, SBLK = early(512), early(1024), early(256), early(256), early(256)
        SBLKn = early(256)
        biasSm, TOEP = early(NKEY), early(384)
        qiTs = early(512).rearrange("p (b x) -> p b x", b=8)

        X = sb("X", 6144)
        hx = X[:, :].rearrange("p (t d) -> p t d", t=3)
        Kt = X[:, 0:2048]
        biasT = X[:, 2048:4096].rearrange("p (h k) -> p h k", h=8)
        workS = X[:, 4096:4096 + NKEY]
        workP = X[:, 5136:5136 + 512].rearrange("p (t k) -> p t k", t=2)
        nT_ = sb("nT_", KT * NT)
        nT = nT_[:, :].rearrange("p (k t) -> p k t", k=KT)
        stageK = nT_[:, 0:4096]
        moT = nT_[:, 0:4 * NT].rearrange("p (h t) -> p h t", h=4)
        C_ = sb("C_", KT * NT)
        mixT = C_[:, :].rearrange("p (k t) -> p k t", k=KT)
        memT = C_[:, 0:4096].rearrange("p (k t) -> p k t", k=KT)
        XN = sb("XN", 4400)
        xn = XN[:, 0:4096].rearrange("p (b d) -> p b d", b=2)

        def normed_rows(stage, t):
            return C_[:, 0:D] if (stage, t) == (2, 2) else xn[:, t % 2, :]
        PB = XN[:, 0:2 * NKEY].rearrange("p (b k) -> p b k", b=2)
        PTs = XN[:, 2 * NKEY:2 * NKEY + 2304].rearrange("p (b k) -> p b k", b=2)
        bkt = XN[:, 0:BUCKET_COLS]
        NAT = sb("NAT", 2048)
        nat = NAT[:, :].rearrange("p (s t c) -> p s t c", s=2, t=2)
        natS = sb("natS", 256)
        SQ = sb("SQ", 1024)
        mkT = sb("mkT", 1024)
        mv = sb("mv", 1024)
        mqT, MQZ = C_[:, 2048:3072], C_[:, 3072:4096]
        vS = sb("vS", 256)
        kTs = sb("kTs", 64)
        gh = sb("gh", 512)
        gcol = sb("gcol", 64)
        cst = sb("cst", NCONST)
        small = sb("small", 512)
        ids = sb("ids", 128, I32)
        relS = sb("relS", 64)
        wiP = sb("wiP", 48)
        abP = sb("abP", 16)
        wsS = sb("wsS", 16)
        top8 = sb("top8", 16)
        route, routeW, routeB = NAT[:, 0:1024], NAT[:, 1024:1536], NAT[:, 1536:1556]
        logitT = SQ[:, 0:NT]

        def cc(name, rows=128):
            at, w = CONST_COLS[name]
            return cst[0:rows, at:at + w]
        ident = cc("ident")
        PS = ctx.enter_context(nc.psum_tensor("PS", [128, 8, 512], F32))

        toep = dram("toep", [8, 128, 385])
        nsc = dram("nsc", [NT, D])
        ysc = dram("ysc", [NBLK * CAP, D])


        sems = {}

        def S(name):
            if name not in sems:
                sems[name] = ctx.enter_context(nc.semaphore(name))
            return sems[name]

        def kview(w):
            return w.rearrange("(p k) n -> p k n", p=128)
        win_v = kview(w_in[0])
        wout_v, wo_v = (w[0].rearrange("(k p) n -> p k n", p=128) for w in (w_out, mem_wo))
        ITEMS = [("in", c, win_v[:, :, c * 512:min(c * 512 + 512, w_in.shape[2])]) for c in CHUNKS[:6]]
        ITEMS += [("mk", 0, kview(mem_wk[0])), ("mv", 0, kview(mem_wv[0]))]
        ITEMS += [("in", c, win_v[:, :, c * 512:c * 512 + 512]) for c in CHUNKS[6:]]
        ITEMS += [("out", c, wout_v[:, :, c * 512:c * 512 + 512]) for c in range(4)]
        ITEMS += [("mq", 0, kview(mem_wq[0]))]
        ITEM_OF = {(k, c): n for n, (k, c, _) in enumerate(ITEMS)}
        NITEM = len(ITEMS)
        N_OUT, N_MQ = ITEM_OF["out", 0], ITEM_OF["mq", 0]
        GROUPS = {("in", 9): 1, ("in", 7): 3, ("in", 8): 3, ("in", 6): 2, ("in", 4): 3, ("in", 5): 3,
                  ("in", 0): 3, ("in", 1): 3, ("mk", 0): 2, ("mq", 0): 3}
        AFTER = {n: ([("item", n - 1)] if ITEMS[n - 1][:2] in GROUPS else []) for n in range(1, N_OUT)}
        AFTER[0] = []
        AFTER[3] += ["index_weights", "index_prompt", "index_sample"]
        AFTER[9] += ["spatial_weights"]
        AFTER[10] += ["spatial"]
        AFTER[N_OUT - 1] += [("item", N_OUT - 1)]
        READERS = {("in", 9): 2, ("in", 6): 5, ("mk", 0): 1}
        RAW_ITEMS = (("in", 9), ("in", 7), ("in", 8))
        STEP_GROUPS = dict(index_weights=1, index_prompt=16, index_sample=8, spatial_weights=3, spatial=5)

        def groups_through(step):
            count = 0
            for n in range(N_OUT):
                for what in AFTER[n]:
                    count += STEP_GROUPS[what] if isinstance(what, str) else GROUPS[ITEMS[what[1]][:2]]
                    if what == step:
                        return count
        UNITS = [(t, h, 128 * (t + 1)) for t in range(2) for h in range(8)]

        RELU = XN[:, 0:1024].rearrange("p (b k) -> p b k", b=2)
        RELS = XN[0:64, 2048:2048 + 2 * NKEY].rearrange("p (b k) -> p b k", b=2)
        wiS = small[0:R, 0:64]
        wiM = small[0:64, 64:96]
        xss, xrs = small[:, 160:163], small[:, 163:166]
        gsum, gx, gt, grs = (small[:, 96 + 16 * i:112 + 16 * i] for i in range(4))
        st_max, st_neg, st_sum, st_inv = (small[:, 168 + 4 * i:172 + 4 * i] for i in range(4))
        rx, rt = small[:, 190:193], small[:, 193:196]
        sq_sums = small[:, 200:212].rearrange("p (t c) -> p t c", t=3)
        PN = sb("PN", 64)
        relR, relX = relS[:, 0:8], relS[:, 8:40]
        abS = abP[:, 8:10]
        memX = stageM.rearrange("p (t d) -> p t d", t=2)
        idxP = stageM.rearrange("p (b r x) -> p b r x", b=8, r=4)
        kiTc = Kt[:, 0:1024].rearrange("p (b k) -> p b k", b=2)
        wsN = Kt[:, 0:1024].rearrange("p (g s) -> p g s", g=8)
        wsT = Kt[:, 1024:2048].rearrange("p (g s) -> p g s", g=8)
        gidx = ids[:, 0:8]
        kg = stageK.rearrange("p (b r c d) -> p b r c d", b=2, r=8, c=2)

        def values(b):
            return (stageM, stageK)[b % 4 // 2][:, 2048 * (b % 2):2048 * (b % 2) + 2048]
        KtH = Kt.rearrange("p (c k) -> p c k", c=2)
        QZv = QZ[:, :].rearrange("p (b c x) -> p b c x", b=8, c=2)
        MQZv = MQZ[:, :].rearrange("p (b h x) -> p b h x", b=8, h=4)
        PSF = PS[:, :, :].rearrange("p b n -> p (b n)")
        mvv = mv[:, :].rearrange("p (t c) -> p t c", t=2)
        mkTv = mkT[:, :].rearrange("p (h k) -> p h k", h=4)
        mqTv = mqT[:, :].rearrange("p (h t) -> p h t", h=4)
        SQv = SQ[:, :].rearrange("p (u k) -> p u k", u=4)
        PTU = XN[:, 3584:4096].rearrange("p (u c k) -> p u c k", u=2, c=2)

        def mem_keys(b):
            at = b % 5
            x = XN[:, 1024 * at:1024 * at + 1024] if at < 2 else nT_[:, 4 * NT + 1024 * (at - 2):4 * NT + 1024 * (at - 1)]
            return x.rearrange("p (h k) -> p h k", h=4)

        def mem_values(b):
            at = b % 6
            x = C_[:, 1024 * at:1024 * at + 1024] if at < 2 else stageM[:, 1024 * (at - 2):1024 * (at - 1)]
            return x.rearrange("p (r c) -> p r c", r=2)
        PBm = XN[:, 2048:2304]
        PTm = XN[:, 2304:2560].rearrange("p (r k) -> p r k", r=2)
        kmg = stageM.rearrange("p (b r c) -> p b r c", b=4, r=2)
        KEYCUT = ((0, 512), (512, 1024), (1024, NKEY))
        AXX = AX.X

        WHERE = (3, 4, 5, 2, 0, 1)
        ring_at = [ring[:, MSLOT * i:MSLOT * (i + 1)] for i in WHERE]
        gate_v, up_v = (w[0].rearrange("e (p k) n -> e p (k n)", p=128) for w in (w_gate, w_up))
        down_v = w_down[0].rearrange("e (p k) n -> e p (k n)", p=128)
        LOTS = ((gate_v, 0), (up_v, 0), (gate_v, 1), (up_v, 1), (down_v, 0), (down_v, 1))
        xg = nT_[:, 0:4096].rearrange("p (b d) -> p b d", b=2)
        XT = C_[:, 0:1024].rearrange("p (k r) -> p k r", k=KT)
        sg, hid = C_[:, 1024:1536], C_[:, 1536:2048]
        hT = C_[:, 2048:2304].rearrange("p (f r) -> p f r", f=4)
        ysb = XN[:, 0:2048].rearrange("p (b x) -> p b x", b=2)
        tabS = sb("tabS", NBLK, U32)
        ids_row = [ids[:, 80 + 3 * i:83 + 3 * i].bitcast(U32) for i in range(2)]
        ids_nov, ids_exp = ids[0:1, 90:91], ids[0:1, 91:91 + NOVF]
        ids_slot, ids_blk = ids[:, 80:86], ids[:, 108:114]
        row_hot = SQ[:, 288:288 + 6 * CAP].rearrange("p (n r) -> p n r", n=6)
        blk_tok = SQ[:, 288 + 6 * CAP:288 + 6 * (CAP + NBLK)].rearrange("p (n b) -> p n b", n=6)
        G = [ring[:, D * i:D * (i + 1)] for i in range(6)]
        UNITS_M = [(t, h, 256) for t in range(2) for h in range(4)]
        NLOT = NEXP * 6
        r_at = [0]

        def r(*shape):
            w = int(np.prod(shape))
            v = route[:, r_at[0]:r_at[0] + w]
            r_at[0] += w
            return v if len(shape) == 1 else v.rearrange("p (t n) -> p t n", t=shape[0])
        LG, AP3, AS, rank = r(3, 20), r(3, 16), r(3, 16), r(3, 16)
        AA = [r(3, 16) for _ in range(2)]
        RX, e_hot = [r(3, 4) for _ in range(2)], [r(3, 4) for _ in range(2)]
        g_hot, r_desc = r(3, 4), r(4)
        r_max, r_sum, g_gate, r_rank, r_first, r_over = (r(3) for _ in range(6))
        e_val, w_tok = [r(3) for _ in range(2)], [r(3) for _ in range(2)]
        extra, first_row, over_row = r(16), r(16), r(16)
        r_blk, r_row = r(6), r(6)
        before = [r(16) for _ in range(2)]
        own_lo, own_hi = r(128)[0:1, :], r(128)[0:1, :]
        r_own = r(8)[0:1, :]
        SQUARES = (3, 15, 27)
        h_count = ITEM_OF["mq", 0] * 4 + 4

        block = ctx.enter_context(nc.Block())

        class Chain:

            def __init__(self, eng, name):
                self.eng, self.sem, self.n = eng, S(name), 0

            def __call__(self, ins):
                self.n += 1
                ins.then_inc(self.sem, 1)
                self.eng.wait_ge(self.sem, self.n)

        def item_normed(eng, n):
            done = [m for m in range(NITEM) if ITEMS[m][0] not in ("mv", "out") and ITEMS[m][:2] not in RAW_ITEMS]
            eng.wait_ge(S("normed"), done.index(n) + 1)

        def bc(ap, axis, shape):
            return ap.unsqueeze(axis).broadcast_to(shape)

        @block.sync
        def _(sp):
            for t in range(2):
                sp.dma_start(hx[:, t, :], x_prompt[0, t * 128:(t + 1) * 128, :]).then_inc(S(f"x_in{t}"), 16)
            sp.dma_start(hx[0:R, 2, :], x_sample.rearrange("b s d -> (b s) d")).then_inc(S("x_in2"), 16)
            for t in range(2):
                sp.dma_start(memX[:, t, :], mem_prompt[0, t * 128:(t + 1) * 128, :]).then_inc(S(f"mem_in{t}"), 16)
            n = 0
            for kind, c, wv in ITEMS + [("wo", c, wo_v[:, :, c * 512:(c + 1) * 512]) for c in range(4)]:
                for q in range(4 if kind != "wo" else 1):
                    if n >= NSLOT:
                        sp.wait_ge(S("ring_free"), n - NSLOT + 1)
                    sp.dma_start(slot(n)[:, :, 0:wv.shape[2]], wv[:, 4 * q:4 * q + 4, :])\
                        .then_inc(S(f"ring_in{n % NSLOT}"), 16)
                    n += 1

            sp.wait_ge(S("stored_in6"), 16 * 5)
            with sp.Fori(0, NEXP) as e:
                for i, (wv, part) in enumerate(LOTS):
                        sp.wait_ge(S("moe_free"), e * 6 + (i + 1))
                        sp.dma_start(ring_at[i], wv[e, :, part * MSLOT:(part + 1) * MSLOT])\
                            .then_inc(S(f"moe_in{i}"), 16)
            sp.wait_ge(S("route_ready"), 1)
            nov = sp.value_load(ids_nov, min_val=0, max_val=NOVF)
            with sp.Fori(0, NOVF) as b:
                with sp.If(b < nov):
                    e = sp.value_load(ids[0:1, bass.ds(b + 91, 1)], min_val=0, max_val=NEXP - 1)
                    for i, (wv, part) in enumerate(LOTS):
                        sp.wait_ge(S("moe_free"), b * 6 + (NLOT + i + 1))
                        sp.dma_start(ring_at[i], wv[e, :, part * MSLOT:(part + 1) * MSLOT])\
                            .then_inc(S(f"moe_in{i}"), 16)
            for t in range(3):
                sp.wait_ge(S("y_ready"), t + 1)
                out = y_prompt[0, t * 128:t * 128 + 128, :] if t < 2 else y_sample.rearrange("b s d -> (b s) d")
                sp.dma_start(out, hx[0:ROWS[t], t, :]).then_inc(S("y_stored"), 16)
            sp.wait_ge(S("y_stored"), 48)

        @block.gpsimd
        def _(pool):
            nc.gpsimd.memset(mv[:, :], 0.0).then_inc(S("zero_ready"), 1)
            pool.wait_ge(S("zero_ready"), 1)
            spare = ysc[NEXP * CAP:NBLK * CAP, :].rearrange("(p r) (h c) -> p r h c", p=128, h=2)
            for q in range(NOVF * CAP // 128 * 2):
                pool.dma_start(spare[:, q // 2, q % 2, :], mv[:, :]).then_inc(S("spare_zero"), 16)
            pool.wait_ge(S("gidx_ready"), 1)
            pool.wait_ge(S("mtr_ready"), 8)
            ik = cache_idx_k[0].rearrange("n (i r) d -> (n i) (r d)", r=8)
            ck = cache_k[0].rearrange("n (i r) c d -> (n i) (r c d)", r=8)
            cv = cache_v[0].rearrange("n (i r) c d -> (n i) (r c d)", r=8)

            def gather(out, table, b, done):
                nc.gpsimd.indirect_dma_start(out, None, table, bass.IndirectOffsetOnAxis(ap=gidx[:, b:b + 1], axis=0))\
                    .then_inc(S(done), 16)
            for b in range(8):
                gather(stageM[:, 512 * b:512 * b + 512], ik, b, "idx_in")
            pool.wait_ge(S("idx_raw"), 8)
            pool.dma_start(wsN, a_ws[0].rearrange("g t s -> t g s")).then_inc(S("wsn_in"), 16)
            pool.wait_ge(S("ring_free"), 4 * N_OUT)
            for b in range(8):
                if b >= 2:
                    pool.wait_ge(S("kt_ready"), 4 * (b - 1))
                gather(stageK[:, 2048 * (b % 2):2048 * (b % 2) + 2048], ck, b, f"k_in{b % 2}")
                if b < 2:
                    gather(values(b), cv, b, f"v_in{b}")
            for b in (2, 3):
                pool.wait_ge(S("kt_ready"), 4 * (b + 5))
                gather(values(b), cv, b, f"v_in{b}")
            pool.wait_ge(S("s_logits"), 2)
            for t in range(2):
                pool.dma_start(hx[:, t, :], x_prompt[0, t * 128:(t + 1) * 128, :]).then_inc(S("h_in"), 16)
            pool.dma_start(hx[0:R, 2, :], x_sample.rearrange("b s d -> (b s) d")).then_inc(S("h_in"), 16)
            for b in range(4, 8):
                pool.wait_ge(S("s_o"), b - 3)
                gather(values(b), cv, b, f"v_in{b % 4}")
            def load_mem_values(b):
                pool.dma_start(mem_values(b).rearrange("p r c -> p (r c)"),
                               cache_mem_v[0, b].rearrange("(p r) h d -> p (r h d)", p=128)).then_inc(S(f"mv_in{b % 6}"), 16)
            pool.wait_ge(S("s_o"), 8)
            for b in range(8):
                if b >= 4:
                    pool.wait_ge(S("kt_ready"), 40 + 2 * (b - 3))
                pool.dma_start(kmg[:, b % 4, :, :].rearrange("p r c -> p (r c)"),
                               cache_mem_k[0, b].rearrange("(p r) h d -> p (r h d)", p=128)).then_inc(S(f"mk_in{b % 4}"), 16)
                if b < 2:
                    pool.wait_ge(S("ring_free"), 4 * (N_OUT + 4))
                    load_mem_values(b)
            for b in range(2, 8):
                if b < 6:
                    pool.wait_ge(S("kt_ready"), 40 + 2 * (b + 3))
                else:
                    pool.wait_ge(S("m_o"), b - 5)
                load_mem_values(b)
            for t in range(3):
                pool.wait_ge(S("xnorm"), 6 + t + 1)
                pool.dma_start(nsc[t * 128:t * 128 + ROWS[t], :], normed_rows(2, t)[0:ROWS[t], :]).then_inc(S(f"n_out{t}"), 16)
            for t in range(3):
                pool.wait_ge(S(f"n_out{t}"), 16)
            pool.wait_ge(S("tab_ready"), 1)
            pool.wait_ge(S("r_ready"), 1)

            def block_rows(b, buf, done):
                nc.gpsimd.indirect_dma_start(xg[0:CAP, buf, :], None, nsc,
                                             bass.IndirectOffsetOnAxis(ap=tabS[0:CAP, b:b + 1], axis=0)).then_inc(S(done), 16)
            for e in range(NEXP + 1):
                if e >= 2:
                    pool.wait_ge(S("xt_ready"), e - 1)
                block_rows(e, e % 2, f"xg_in{e % 2}")
            pool.wait_ge(S("route_ready"), 1)
            nov = pool.value_load(ids_nov, min_val=0, max_val=NOVF)
            for b in range(NOVF):
                with pool.If(nov > b):
                    pool.wait_ge(S("xt_ready"), NEXP + b + (b > 0))
                    block_rows(min(NEXP + b + 1, NBLK - 1), 1, "ov_x")
            with pool.If(nov > 0):
                pool.wait_ge(S("ov_stored"), nov * 32 + 32)
            for k in range(2):
                pool.wait_ge(S(f"y_out{k}"), 32 * (NEXP // 2 + 1))
            pool.wait_ge(S("moe_free"), NLOT + 6)
            for t in range(3):
                for i in range(2):
                    nc.gpsimd.indirect_dma_start(G[2 * t + i][0:ROWS[t], :], None, ysc,
                                                 bass.IndirectOffsetOnAxis(ap=ids_row[i][0:ROWS[t], t:t + 1], axis=0))\
                        .then_inc(S(f"g_in{t}"), 16)

        @block.tensor
        def _(pe):
            mm, tr = nc.tensor.matmul, nc.tensor.transpose
            ring_n, misc = [0], [0]

            def acc(n, t):
                return PS[:, 3 * (n % 2) + t, :]

            def transpose_rows(stage, src):
                for t in range(3):
                    pe.wait_ge(S("xnorm"), 3 * stage + t + 1)
                    for q in range(4):
                        g = 4 * t + q
                        if g >= 4:
                            pe.wait_ge(S("tr_free"), 12 * stage + g - 3)
                        for i in range(4):
                            last = tr(PS[:, g % 4, 128 * i:128 * i + ROWS[t]],
                                      src(t)[0:ROWS[t], 4 * q + i:D:KT],
                                      ident[0:ROWS[t], 0:ROWS[t]])
                        last.then_inc(S("tr_ready"), 1)

            def strips(lhs, kt, n, ws, width, st, sp_):
                for j in range(4 if width == 512 else 1):
                    last = mm(acc(n, 2)[32 * j:32 * j + 32, 0:min(width, 128)], lhs[:, kt, T:NT],
                              ws[:, 128 * j:min(128 * j + 128, width)], start=st, stop=sp_)
                return last

            def products(n):
                kind, c, wv = ITEMS[n]
                width = wv.shape[2]
                lhs = {"in": nT, "mk": memT, "mv": memT, "out": mixT, "mq": nT}[kind]
                if 2 <= n < N_OUT:
                    pe.wait_ge(S("evac"), n - 1)
                if n >= N_OUT + 2 and kind == "out":
                    pe.wait_ge(S("h_add"), n - N_OUT - 1)
                for kt in range(KT):
                    if kt % 4 == 0:
                        m = ring_n[0]
                        pe.wait_ge(S(f"ring_in{m % NSLOT}"), 16 * (m // NSLOT + 1))
                    ws = slot(m)[:, kt % 4, 0:width]
                    st, sp_ = kt == 0, kt == KT - 1
                    for t in range(2):
                        last = mm(acc(n, t)[:, 0:width], lhs[:, kt, t * 128:(t + 1) * 128], ws, start=st, stop=sp_)
                    if lhs is not memT:
                        last = strips(lhs, kt, n, ws, width, st, sp_)
                    if kt % 4 == 3:
                        last.then_inc(S("ring_free"), 1)
                        ring_n[0] += 1

            def group():
                n = misc[0]
                misc[0] += 1
                if n >= 2:
                    pe.wait_ge(S("misc_free"), n - 1)
                return PS[:, 6 + n % 2, :]

            def done(last):
                last.then_inc(S("misc_ready"), 1)

            def item_transposes(n):
                key, b = ITEMS[n][:2], n % 2
                if key in RAW_ITEMS:
                    pe.wait_ge(S("evac"), n + 1)
                else:
                    item_normed(pe, n)
                if key == ("in", 9):
                    bank = group()
                    for t in range(3):
                        src = nat[:, b, t, 0:128] if t < 2 else natS[0:R, b * 128:b * 128 + 128]
                        last = tr(bank[:, t * 128:t * 128 + ROWS[t]], src, ident[0:ROWS[t], 0:ROWS[t]])
                    done(last)
                    return
                if key == ("in", 6):
                    bank = group()
                    for h in range(2):
                        for t in range(2):
                            last = tr(bank[:, h * 256 + t * 128:h * 256 + t * 128 + 128],
                                      nat[:, b, t, h * 128:h * 128 + 128], ident)
                    done(last)
                else:
                    for t in range(2):
                        bank = group()
                        for j in range(4):
                            last = tr(bank[:, j * 128:j * 128 + 128], nat[:, b, t, j * 128:j * 128 + 128], ident)
                        done(last)
                if key[0] != "mk":
                    bank = group()
                    done(tr(bank[:, 0:128], natS[:, b * 128:b * 128 + 128], ident))

            def index_weights():
                bank = group()
                done(mm(bank[0:64, 0:R], wiS, ident[0:R, 0:R], start=True, stop=True))

            def index_prompt():
                pe.wait_ge(S("misc_free"), misc[0] - 1)
                for t in range(2):
                    nk = 128 * (t + 1)
                    for pair in range(4):
                        banks = (group(), group())
                        for i in range(2):
                            for odd in range(2):
                                rows = slice(64 * odd, 64 * odd + 64)
                                last = mm(banks[odd][:, i * 256:i * 256 + nk],
                                          qiT[rows, 2 * pair + i, t * 128:t * 128 + 128], kiT[rows, 0:nk],
                                          start=True, stop=True)
                                if i == 1:
                                    done(last)

            def index_sample():
                pe.wait_ge(S("evac"), 4)
                pe.wait_ge(S("wz_ready"), 1)

                def weigh(b):
                    pe.wait_ge(S("idx_relu"), b + 1)
                    for i, (a, z) in enumerate(KEYCUT):
                        last = mm(PS[0:R, 3 + i, 0:z - a], Wz[0:64, b * 32:b * 32 + 32],
                                  RELS[:, b % 2, a:z], start=b == 0, stop=b == 7)
                    last.then_inc(S("idx_sum"), 1)
                for b in range(8):
                    pe.wait_ge(S("idx_in"), 16 * 8)
                    bank = group()
                    for i in range(4):
                        last = tr(bank[:, i * 128:i * 128 + 128], idxP[:, b, i, :], ident)
                    done(last)
                    if b:
                        weigh(b - 1)
                    pe.wait_ge(S("misc_free"), misc[0])
                    for odd in range(2):
                        rows = slice(64 * odd, 64 * odd + 64)
                        mm(PS[0:64, odd, :], qiTs[rows, b, :], kiTc[rows, b % 2, :], start=True, stop=True)
                    mm(PS[0:64, 2, 0:NS], qiTs[0:64, b, :], kiT[0:64, T + NS * b:T + NS * b + NS],
                       start=True, stop=True).then_inc(S("idx_raw"), 1)
                weigh(7)
                pe.wait_ge(S("scoreS"), 1)

            def spatial_weights():
                pe.wait_ge(S("ws_masked"), 1)
                pe.wait_ge(S("sblk_ready"), 1)
                for half in range(2):
                    bank = group()
                    for i in range(4):
                        last = tr(bank[:, i * 128:i * 128 + 128], wsN[:, 4 * half + i, :], ident)
                    done(last)
                bank = group()
                for c in range(2):
                    last = tr(bank[:, c * 128:c * 128 + 128], SBLKn[:, c * 128:c * 128 + 128], ident)
                done(last)

            def spatial():
                item_normed(pe, ITEM_OF["in", 3])
                pe.wait_ge(S("misc_free"), misc[0])
                for pair in range(4):
                    bank = group()
                    for i in range(2):
                        g = 2 * pair + i
                        last = mm(bank[:, i * 256:i * 256 + 256], wsT[:, g, :], vn[:, :, g * 128:g * 128 + 128],
                                  start=True, stop=True)
                    done(last)
                bank = group()
                for c in range(2):
                    last = mm(bank[:, c * 128:c * 128 + 128], SBLK[:, c * 128:c * 128 + 128], vnS[:, c, :],
                              start=True, stop=True)
                done(last)

            pe.wait_ge(S("cst_in"), 16)
            transpose_rows(0, lambda t: hx[:, t, :])
            for t in range(2):
                pe.wait_ge(S(f"mem_in{t}"), 16)
                for q in range(4):
                    g = 4 * t + q
                    if g >= 4:
                        pe.wait_ge(S("mtr_free"), g - 3)
                    for i in range(4):
                        last = tr(PS[:, 4 + g % 4, 128 * i:128 * i + 128],
                                  memX[:, t, 4 * q + i:D:KT], ident)
                    last.then_inc(S("mtr_ready"), 1)
            pe.wait_ge(S("tr_free"), 12)
            pe.wait_ge(S("mtr_free"), 8)
            pe.wait_ge(S("bkt_in"), 16)
            pe.wait_ge(S("rel_ready"), 1)
            mm(PS[0:8, 6, 0:384], relR[0:32, :], bkt[0:32, NKEY:NKEY + 384], start=True, stop=True)
            for i, (a, z) in enumerate(KEYCUT):
                last = mm(PS[0:R, i, 0:z - a], relX, bkt[:, a:z], start=True, stop=True)
            last.then_inc(S("bias_ready"), 1)
            pe.wait_ge(S("bias_free"), 1)
            steps = dict(index_weights=index_weights, index_prompt=index_prompt, index_sample=index_sample,
                         spatial_weights=spatial_weights, spatial=spatial)
            for n in range(N_OUT):
                products(n)
                for what in AFTER[n]:
                    steps[what]() if isinstance(what, str) else item_transposes(what[1])

            def unit_attention(base, units, scores, out):
                for u in range(len(units) + 4):
                    if u < len(units):
                        if u >= 2:
                            pe.wait_ge(S("unit_added"), base + u - 1)
                        scores(u, PS[:, u % 2, :]).then_inc(S("unit_s"), 1)
                    v = u - 3
                    if 0 <= v < len(units):
                        nk = units[v][2]
                        pe.wait_ge(S("unit_normed"), base + v + 1)
                        if v >= 2:
                            pe.wait_ge(S("unit_pt_free"), base + v - 1)
                        for c in range(nk // 128):
                            last = tr(PS[:, 2 + v % 2, c * 128:c * 128 + 128],
                                      SQv[:, v % 4, c * 128:c * 128 + 128], ident)
                        last.then_inc(S("unit_pt"), 1)
                    v = u - 4
                    if 0 <= v < len(units):
                        pe.wait_ge(S("unit_pt_free"), base + v + 1)
                        if v >= 2:
                            pe.wait_ge(S("unit_o_free"), base + v - 1)
                        nk = units[v][2]
                        for c in range(nk // 128):
                            last = mm(PS[:, 4 + v % 2, 0:128], out(v, c), PTU[:, v % 2, c, :],
                                      start=c == 0, stop=c == nk // 128 - 1)
                        last.then_inc(S("unit_o"), 1)

            pe.wait_ge(S("misc_free"), misc[0])
            pe.wait_ge(S("evac"), N_OUT)

            def own_scores(u, bank):
                t, h, nk = UNITS[u]
                return mm(bank[:, 0:nk], qT[:, h, t * 128:t * 128 + 128], kT[:, h // 4, 0:nk], start=True, stop=True)
            unit_attention(0, UNITS, own_scores,
                           lambda v, c: vP[:, c, UNITS[v][1] // 4 * 128:UNITS[v][1] // 4 * 128 + 128])
            pe.wait_ge(S("unit_o_free"), len(UNITS))

            groups = [0]

            def kgroup():
                g = groups[0]
                groups[0] += 1
                if g >= 2:
                    pe.wait_ge(S("kt_free"), g - 1)
                return PS[:, 6 + g % 2, :]
            pe.wait_ge(S("topkS"), 1)
            for b in range(8):
                pe.wait_ge(S(f"k_in{b % 2}"), 16 * (b // 2 + 1))
                for c in range(2):
                    for half in range(2):
                        bank = kgroup()
                        for i in range(4):
                            last = tr(bank[:, i * 128:i * 128 + 128], kg[:, b % 2, 4 * half + i, c, :], ident)
                        last.then_inc(S("kt_ready"), 1)
                pe.wait_ge(S("kt_free"), 4 * (b + 1))
                rows = slice(32 * (b % 4), 32 * (b % 4) + 32)
                for c in range(2):
                    for i, (a, z) in enumerate(KEYCUT):
                        keys = KtH[:, c, a:z] if i < 2 else kTs[:, c * 32 + 4 * b:c * 32 + 4 * b + 4]
                        last = mm(PS[rows, 3 * (b // 4) + i, 0:z - a], QZv[:, b, c, :], keys, start=c == 0, stop=False)
                last.then_inc(S("s_qk"), 1)
                if b % 4 == 3:
                    for what in range(2):
                        for i, (a, z) in enumerate(KEYCUT):
                            for d in range(b - 3, b + 1):
                                lhs = (cc("ident", R)[:, 0:R], cc("pick", R)[:, 32 * d:32 * d + 32])[what]
                                last = mm(PS[32 * (d % 4):32 * (d % 4) + 32, 3 * (b // 4) + i, 0:z - a], lhs,
                                          (biasSm[0:R, a:z], workS[0:R, a:z])[what], start=False, stop=what == 1)
                    last.then_inc(S("s_logits"), 1)
            for x in range(2):
                pe.wait_ge(S("s_probs"), x + 1)
                for g in range(3):
                    bank = kgroup()
                    if g < 2:
                        for i in range(4):
                            r = 4 * g + i
                            last = tr(bank[:, i * 128:i * 128 + 128], PB[:, x, r:PAST:8], ident)
                    else:
                        last = tr(bank[0:R, 0:128], PN[:, x * 32:x * 32 + 32], ident)
                    last.then_inc(S("kt_ready"), 1)
                pe.wait_ge(S("kt_free"), groups[0])
                for b in range(4 * x, 4 * x + 4):
                    pe.wait_ge(S(f"v_in{b % 4}"), 16 * (b // 4 + 1))
                    rows = 32 * (b % 4)
                    out = PS[rows:rows + 32, x, 0:256]
                    for r in range(8):
                        mm(out, PTs[:, x, r * 128 + rows:r * 128 + rows + 32], values(b)[:, 256 * r:256 * r + 256],
                           start=r == 0, stop=False)
                    mm(out, PTs[0:R, x, 1024 + rows:1024 + rows + 32], vS[0:R, :], start=False, stop=True)\
                        .then_inc(S("s_o"), 1)
            for x in range(2):
                pe.wait_ge(S("s_o_sb"), x + 1)
                bank = kgroup()
                for c in range(2):
                    last = tr(bank[:, 128 * c:128 * c + 128], SQ[:, 256 * x + 128 * c:256 * x + 128 * c + 128], ident)
                last.then_inc(S("kt_ready"), 1)
            pe.wait_ge(S("kt_free"), groups[0])
            pe.nop().then_inc(S("moe_free"), 3)
            for n in range(N_OUT, N_MQ):
                products(n)
            transpose_rows(1, lambda t: normed_rows(1, t))
            pe.wait_ge(S("tr_free"), 24)
            products(N_MQ)

            def mem_key_transposes(b):
                pe.wait_ge(S(f"mk_in{b % 4}"), 16 * (b // 4 + 1))
                for r in range(2):
                    bank = kgroup()
                    for h in range(4):
                        last = tr(bank[:, h * 128:h * 128 + 128], kmg[:, b % 4, r, h * 128:h * 128 + 128], ident)
                    last.then_inc(S("kt_ready"), 1)
            for b in range(4):
                mem_key_transposes(b)
            pe.wait_ge(S("kt_free"), groups[0])
            item_transposes(N_MQ)
            pe.wait_ge(S("misc_free"), misc[0])

            def mem_scores(u, bank):
                t, h, _ = UNITS_M[u]
                return mm(bank[:, 0:256], mqTv[:, h, t * 128:t * 128 + 128], mkTv[:, h, :], start=True, stop=True)
            unit_attention(len(UNITS), UNITS_M, mem_scores,
                           lambda v, c: mvv[:, c, UNITS_M[v][1] * 128:UNITS_M[v][1] * 128 + 128])
            pe.wait_ge(S("unit_o_free"), len(UNITS) + len(UNITS_M))
            for b in range(8):
                if b >= 4:
                    mem_key_transposes(b)
                    pe.wait_ge(S("kt_free"), groups[0])
                for h in range(4):
                    last = mm(PS[32 * (b // 2):32 * (b // 2) + 32, 0, 0:256], MQZv[:, b, h, :], mem_keys(b)[:, h, :],
                              start=b % 2 == 0 and h == 0, stop=b % 2 == 1 and h == 3)
                last.then_inc(S("m_qk"), 1)
            pe.wait_ge(S("m_probs"), 1)
            bank = kgroup()
            for r in range(2):
                last = tr(bank[:, r * 128:r * 128 + 128], PBm[:, r * 128:r * 128 + 128], ident)
            last.then_inc(S("kt_ready"), 1)
            pe.wait_ge(S("kt_free"), groups[0])
            for b in range(8):
                pe.wait_ge(S(f"mv_in{b % 6}"), 16 * (b // 6 + 1))
                rows = 32 * (b // 2)
                for r in range(2):
                    last = mm(PS[rows:rows + 32, 1 + b % 2, :], PTm[:, r, rows:rows + 32], mem_values(b)[:, r, :],
                              start=r == 0, stop=r == 1)
                last.then_inc(S("m_o"), 1)
            pe.wait_ge(S("m_o_sb"), 1)
            pe.nop().then_inc(S("moe_free"), 1)
            for z in range(2):
                bank = kgroup()
                for h in range(4):
                    last = tr(bank[:, 128 * h:128 * h + 128], SQ[:, 512 * z + 128 * h:512 * z + 128 * h + 128], ident)
                last.then_inc(S("kt_ready"), 1)
            pe.wait_ge(S("kt_free"), groups[0])
            for c in range(4):
                m, n = ring_n[0], N_MQ + 1 + c
                if c >= 2:
                    pe.wait_ge(S("h_add"), 4 + c - 1)
                pe.wait_ge(S(f"ring_in{m % NSLOT}"), 16 * (m // NSLOT + 1))
                for kt in range(4):
                    for t in range(2):
                        mm(acc(n, t), moT[:, kt, t * 128:t * 128 + 128], slot(m)[:, kt, :], start=kt == 0, stop=kt == 3)
                    last = strips(moT, kt, n, slot(m)[:, kt, :], 512, kt == 0, kt == 3)
                last.then_inc(S("ring_free"), 1)
                ring_n[0] += 1
            pe.wait_ge(S("h_add"), 8)
            pe.nop().then_inc(S("moe_free"), 2)
            transpose_rows(2, lambda t: normed_rows(2, t))
            pe.wait_ge(S("tr_free"), 36)
            pe.wait_ge(S("routew_in"), 64)
            pe.wait_ge(S("routew_zero"), 1)
            for kt in range(KT):
                j = 32 * (kt % 4)
                last = mm(PS[j:j + 32, 6, 0:NT], routeW[:, 32 * kt:32 * kt + 32], nT[:, kt, :], start=kt < 4, stop=kt >= KT - 4)
            last.then_inc(S("r_sums"), 1)
            pe.wait_ge(S("r_sums_sb"), 1)
            for t in range(3):
                last = mm(PS[0:ROWS[t], 4, 20 * t:20 * t + 20], logitT[:, t * 128:t * 128 + ROWS[t]], cc("fold")[:, 0:20],
                          start=True, stop=True)
            last.then_inc(S("r_ready"), 1)
            pe.wait_ge(S("picked"), 1)
            for t in range(4):
                rows = ROWS[t] if t < 3 else 128
                for u in range(min(t + 1, 3)):
                    lhs = cc("rank" if u == t else "ones", ROWS[u])[:, 0:rows]
                    last = mm(PS[0:rows, 5, 16 * t:16 * t + 16], lhs, AS[0:ROWS[u], u, :],
                              start=u == 0, stop=u == min(t, 2))
            last.then_inc(S("rank_ready"), 1)
            pe.wait_ge(S("hot_ready"), 1)
            for n in range(6):
                rows = ROWS[n % 3]
                last = mm(PS[0:CAP, 7, 0:NBLK], row_hot[0:rows, n, :], blk_tok[0:rows, n, :], start=n == 0, stop=n == 5)
            last.then_inc(S("tab_sum"), 1)

            def rows_t(k):
                for kt in range(KT):
                    put = tr if kt else mm
                    last = put(PS[:, kt // 8, (kt % 8) * 64:(kt % 8) * 64 + 64], xg[0:CAP, k, kt:D:KT], ident[0:CAP, 0:CAP])
                return last

            def gate_up(landed):
                for kt in range(KT):
                    if kt % 8 == 0:
                        landed(2 * (kt // 8))
                        landed(2 * (kt // 8) + 1)
                    for half in range(2):
                        w = ring_at[2 * (kt // 8) + half].rearrange("p (k n) -> p k n", k=8)[:, kt % 8, :]
                        last = mm(PS[64 * half:64 * half + 64, 2, :], XT[:, kt, :], w, start=kt == 0, stop=kt == KT - 1)
                        if kt % 8 == 7:
                            last.then_inc(S("moe_free"), 1)
                return last

            def hidden_t():
                for f in range(4):
                    put = tr if f else mm
                    last = put(PS[:, 3, 64 * f:64 * f + 64], hid[64:128, f:FF:4], cst[64:128, 64:128])
                return last

            def down(landed):
                for f in range(4):
                    if f % 2 == 0:
                        landed(4 + f // 2)
                    for x in range(2):
                        for half in range(2):
                            w = ring_at[4 + f // 2].rearrange("p (k n) -> p k n", k=2)[:, f % 2, half * 1024 + x * 512:half * 1024 + x * 512 + 512]
                            last = mm(PS[64 * half:64 * half + 64, 4 + x, :], hT[:, f, :], w, start=f == 0, stop=f == 3)
                    if f == 1:
                        last.then_inc(S("moe_free"), 1)
                return last

            for name, turn in (("y_out0", 32), ("y_out1", 32), ("y_out_psum", 1), ("ov_stored", 32), ("ov_y_sb", 1)):
                pe.nop().then_inc(S(name), turn)
            pe.wait_ge(S("xg_in0"), 16)
            rows_t(0).then_inc(S("xt_ready"), 1)
            with pe.Fori(0, NEXP // 2) as i:
                for k in range(2):
                    e = i * 2 + k

                    def landed(lot):
                        pe.wait_ge(S(f"moe_in{lot}"), i * 32 + 16 * (k + 1))
                    pe.wait_ge(S("xt_laid"), e + 1)
                    gate_up(landed)
                    pe.wait_ge(S(f"xg_in{1 - k}"), i * 16 + 16 * (1 + k))
                    rows_t(1 - k).then_inc(S("xt_ready"), 1)
                    pe.wait_ge(S("hidden"), e + 1)
                    hidden_t().then_inc(S("ht_ready"), 1)
                    pe.wait_ge(S("ht_laid"), e + 1)
                    pe.wait_ge(S("y_out_psum"), e + 1)
                    down(landed).then_inc(S("moe_free"), 1)
            pe.wait_ge(S("xt_laid"), NEXP + 1)
            pe.wait_ge(S("y_out_psum"), NEXP + 1)
            pe.wait_ge(S("route_ready"), 1)
            nov = pe.value_load(ids_nov, min_val=0, max_val=NOVF)
            with pe.Fori(0, NOVF) as b:
                with pe.If(b < nov):
                    def landed(lot):
                        pe.wait_ge(S(f"moe_in{lot}"), b * 16 + 16 * (NEXP + 1))
                    pe.wait_ge(S("xt_laid"), b + (NEXP + 1))
                    gate_up(landed)
                    pe.wait_ge(S("ov_x"), b * 16 + 16)
                    rows_t(1).then_inc(S("xt_ready"), 1)
                    pe.wait_ge(S("ov_hidden"), b + 1)
                    hidden_t().then_inc(S("ov_ht"), 1)
                    pe.wait_ge(S("ov_ht_laid"), b + 1)
                    pe.wait_ge(S("ov_y_sb"), b + 1)
                    down(landed).then_inc(S("moe_free"), 1)

        @block.scalar
        def _(act):
            A = nc.scalar.activation
            own = Chain(act, "act_step")
            misc = [0]
            for i, g in enumerate((norm_mix, norm_mem, norm_ffn)):
                act.dma_start(gcol[:, 16 * i:16 * i + 16], g[0].rearrange("(p k) -> p k", p=128)).then_inc(S("gcol_in"), 16)
            act.dma_start(cst[:, :], consts).then_inc(S("cst_in"), 16)
            act.dma_start(relR, bass.AP(rel_bias.tensor, 0, [[0, 4], [8, 32], [1, 8]])).then_inc(S("rel_in"), 16)
            act.dma_start(ids[:, 16:80], bass.AP(page_table.tensor, 0, [[0, 128], [1, NB * NPAGE]])).then_inc(S("pt_in"), 16)

            def row_squares():
                for t in range(3):
                    act.wait_ge(S(f"x_in{t}"), 16)
                    if t:
                        act.wait_ge(S("rowsq"), t)
                    A(nT_[0:ROWS[t], 0:D], hx[0:ROWS[t], t, :], ACT.Square,
                      accum_out=xss[0:ROWS[t], t:t + 1]).then_inc(S("rowsq"), 1)

            def chunk_squares(stage):
                for c in range(4):
                    act.wait_ge(S("h_add"), 4 * (stage - 1) + c + 1)
                    for t in range(3):
                        if c:
                            act.wait_ge(S("rowsq"), SQUARES[stage - 1] + 3 * (c - 1) + t + 1)
                        A(nT_[0:ROWS[t], 4 * NT + 512 * t:4 * NT + 512 * t + 512], hx[0:ROWS[t], t, 512 * c:512 * c + 512],
                          ACT.Square, accum_out=sq_sums[0:ROWS[t], t, c:c + 1]).then_inc(S("rowsq"), 1)

            def take():
                n = misc[0]
                misc[0] += 1
                act.wait_ge(S("misc_ready"), n + 1)
                return PS[:, 6 + n % 2, :]

            def gave(last):
                last.then_inc(S("misc_free"), 1)

            def evacuate(n):
                kind, c, _ = ITEMS[n]
                b, ps = n % 2, 3 * (n % 2)
                act.wait_ge(S("ring_free"), 4 * (n + 1))
                if n >= 2:
                    before = ITEMS[n - 2][:2]
                    if before in READERS:
                        act.wait_ge(S(f"stored_{before[0]}{before[1]}"), 16 * READERS[before])
                    if before in (("in", 2), ("in", 3)):
                        item_normed(act, n - 2)
                fn = ACT.Gelu if kind == "in" and c < 4 else ACT.Copy
                if (kind, c) == ("in", 9):
                    for z in range(2):
                        A(nat[:, b, :, 64 * z:64 * z + 64], PS[:, ps:ps + 2, 0:64], ACT.Copy)
                        A(natS[0:R, b * 128 + 64 * z:b * 128 + 64 * z + 64], PS[0:R, ps + 2, 0:64], ACT.Copy)
                    A(wiP[:, 0:32].rearrange("p (t h) -> p t h", t=2), PS[:, ps:ps + 2, 64:80], ACT.Copy,
                      scale=1.0 / 32)
                    A(wiS.rearrange("p (h c q) -> p h c q", h=2, c=8),
                      bc(PS[0:R, ps + 2, 64:80].rearrange("p (c h) -> p h c", h=2), 3, [R, 2, 8, 4]),
                      ACT.Copy, scale=1.0 / 32).then_inc(S("evac"), 1)
                elif kind == "mv":
                    act.wait_ge(S("spare_zero"), NOVF * CAP // 128 * 32)
                    A(mvv, PS[:, ps:ps + 2, :], ACT.Copy).then_inc(S("evac"), 1)
                else:
                    if (kind, c) == ("in", 6):
                        A(vP, PS[:, ps:ps + 2, 256:512], ACT.Copy)
                        for h in range(2):
                            A(vS[0:R, h * 128:h * 128 + 128], PS[64 + 32 * h:96 + 32 * h, ps + 2, 0:128], ACT.Copy)
                    last = A(nat[:, b, :, :], PS[:, ps:ps + 2, :], fn)
                    if kind != "mk":
                        last = A(natS[:, b * 128:b * 128 + 128], PS[:, ps + 2, 0:128], fn)
                    last.then_inc(S("evac"), 1)

            def item_layout(n):
                kind, c, _ = ITEMS[n]
                if (kind, c) == ("in", 9):
                    gave(A(kiT, take()[:, 0:NT], ACT.Copy))
                    return
                if (kind, c) == ("in", 6):
                    gave(A(kT.rearrange("p h t -> p (h t)"), take(), ACT.Copy))
                    gave(A(kTs[:, 0:64], take()[:, 0:64], ACT.Copy))
                    return
                rows = {"mk": lambda: mkTv, "mq": lambda: mqTv,
                        "in": lambda: (qiT[:, 4 * (c - 7):4 * (c - 7) + 4, :] if c in (7, 8) else
                                       qT[:, 4 * (c - 4):4 * (c - 4) + 4, :] if c in (4, 5) else
                                       mixT[:, 4 * c:4 * c + 4, 0:T])}[kind]()
                for t in range(2):
                    bank = take()
                    gave(A(rows[:, :, t * 128:t * 128 + 128], bank.rearrange("p (j k) -> p j k", j=4), ACT.Copy))
                if kind == "mk":
                    return
                bank = take()
                strip = bank[:, 0:128].rearrange("p (j b q) -> p j b q", j=4, b=8)
                if kind == "mq":
                    for h in range(4):
                        for z in range(2):
                            last = A(MQZv[:, z:8:2, h, 16 * z + 4 * h:16 * z + 4 * h + 4],
                                     strip[:, h, z:8:2, :], ACT.Copy)
                    gave(last)
                elif c in (7, 8):
                    for half in range(2):
                        for to in range(2):
                            x = qiTs[64 * to:64 * to + 64, :, 32 * half + 16 * (c - 7):32 * half + 16 * (c - 7) + 16]
                            last = A(x.rearrange("p b (j q) -> p j b q", j=4), strip[64 * half:64 * half + 64], ACT.Copy)
                    gave(last)
                elif c in (4, 5):
                    kv = c - 4
                    gave(A(QZv[:, :, kv, 16 * kv:16 * kv + 16].rearrange("p b (j q) -> p j b q", j=4), strip, ACT.Copy))
                else:
                    gave(A(mixT[:, 4 * c:4 * c + 4, T:NT], bank[:, 0:128].rearrange("p (j k) -> p j k", j=4), ACT.Copy))

            def index_weights():
                gave(A(wiM, take()[0:64, 0:R], ACT.Copy))

            def index_prompt():
                for u in range(16):
                    nk = 128 * (u // 8 + 1)
                    if u >= 2:
                        act.wait_ge(S("idxp_free"), u - 1)
                    bank = take()
                    A(RELU[:, u % 2, :].rearrange("p (h k) -> p h k", h=2)[:, :, 0:nk],
                      bank.rearrange("p (h k) -> p h k", h=2)[:, :, 0:nk], ACT.Relu).then_inc(S("misc_free"), 1)

            def index_sample():
                for b in range(8):
                    if b >= 2:
                        act.wait_ge(S("idx_raw"), b - 1)
                    gave(A(kiTc[:, b % 2, :], take(), ACT.Copy))
                    act.wait_ge(S("idx_raw"), b + 1)
                    if b >= 2:
                        act.wait_ge(S("idx_sum"), b - 1)
                    for odd in range(2):
                        A(RELS[:, b % 2, 0:PAST].rearrange("p (x r z) -> p r x z", r=4, z=2)[:, :, :, odd],
                          PS[0:64, odd, :].rearrange("p (r x) -> p r x", r=4), ACT.Relu)
                    A(RELS[:, b % 2, PAST:NKEY], PS[0:64, 2, 0:NS], ACT.Relu).then_inc(S("idx_relu"), 1)

            def spatial_weights():
                for half in range(2):
                    gave(A(wsT[:, 4 * half:4 * half + 4, :], take().rearrange("p (g t) -> p g t", g=4), ACT.Copy))
                gave(A(SBLK, take()[:, 0:256], ACT.Copy))

            def spatial():
                act.wait_ge(S("ws_in"), 16 * 17)
                store_item(9)
                act.wait_ge(S("stored_in2"), 64)
                act.wait_ge(S("stored_in3"), 64)
                for pair in range(4):
                    bank = take()
                    for i in range(2):
                        g = 2 * pair + i
                        last = A(vn[:, :, g * 128:g * 128 + 128], bank[:, i * 256:i * 256 + 256].rearrange("p (t c) -> p t c", t=2),
                                 ACT.Identity, bias=abP[:, g:g + 1])
                    gave(last)
                bank = take()
                for c in range(2):
                    last = A(vnS[:, c, :], bank[:, c * 128:c * 128 + 128], ACT.Identity, bias=abS[:, c:c + 1])
                gave(last)

            def store_item(n):
                key, b = ITEMS[n][:2], n % 2
                if key in RAW_ITEMS or key == ("mv", 0):
                    act.wait_ge(S("evac"), n + 1)
                else:
                    item_normed(act, n)
                pairs = {("in", 9): lambda: [(o_ki[0, 0].rearrange("(t p) d -> p t d", p=128), nat[:, b, :, 0:64]),
                                             (o_kis[0].rearrange("b s d -> (b s) d"), natS[0:R, b * 128:b * 128 + 64])],
                         ("in", 6): lambda: [(o_k[0, 0].rearrange("(t p) h d -> p t (h d)", p=128), nat[:, b, :, 0:256]),
                                             (o_v[0, 0].rearrange("(t p) h d -> p t (h d)", p=128), vP),
                                             (o_vs[0].rearrange("b s h d -> (b s) (h d)"), vS[0:R, :])] +
                         [(o_ks[0].rearrange("b s h d -> (b s) h d")[:, h, :], natS[32 * h:32 * h + 32, b * 128:b * 128 + 128])
                          for h in range(2)],
                         ("mk", 0): lambda: [(o_mk[0, 0].rearrange("(t p) h d -> p t (h d)", p=128), nat[:, b, :, :])],
                         ("mv", 0): lambda: [(o_mv[0, 0].rearrange("(t p) h d -> p t (h d)", p=128), mvv)],
                         ("in", 2): lambda: vn_rows(0), ("in", 3): lambda: vn_rows(1)}[key]()
                for out, src in pairs:
                    act.dma_start(out, src).then_inc(S(f"stored_{key[0]}{key[1]}"), 16)
                stored.append((f"stored_{key[0]}{key[1]}", 16 * len(pairs)))

            stored = []

            def vn_rows(c):
                rows = o_cvs[0].rearrange("b s g d -> (b s) g d")
                return [(rows[:, 4 * c + j, :], vnS[32 * j:32 * j + 32, c, :]) for j in range(4)]

            row_squares()
            act.dma_start(bkt, buckets).then_inc(S("bkt_in"), 16)
            for g in range(8):
                act.wait_ge(S("mtr_ready"), g + 1)
                t, q = g // 4, g % 4
                A(memT[:, 4 * q:4 * q + 4, t * 128:t * 128 + 128], PS[:, 4 + g % 4, :].rearrange("p (k t) -> p k t", k=4),
                  ACT.Copy).then_inc(S("mtr_free"), 1)
            act.wait_ge(S("bias_ready"), 1)
            own(A(TOEP[0:8, :], PS[0:8, 6, 0:384], ACT.Copy))
            A(biasSm[0:R, :], PSF[0:R, 0:NKEY], ACT.Copy).then_inc(S("bias_free"), 1)
            act.dma_start(toep[:, :, 0:384], bc(TOEP[0:8, :], 1, [8, 128, 384])).then_inc(S("toep_out"), 16)
            for i, g in enumerate((b_qnorm, b_knorm, mem_qnorm, mem_knorm)):
                act.dma_start(gh[:, 128 * i:128 * i + 128], bass.AP(g.tensor, 0, [[0, 128], [1, 128]])).then_inc(S("gh_in"), 16)
            act.dma_start(gav[:, :], bass.AP(a_vnorm.tensor, 0, [[0, 128], [1, 1024]])).then_inc(S("gh_in"), 16)
            for j in range(4):
                act.dma_start(gavS[32 * j:32 * j + 32, :].rearrange("p (c d) -> p c d", c=2),
                              bass.AP(a_vnorm.tensor, 128 * j, [[0, 32], [512, 2], [1, 128]])).then_inc(S("gh_in"), 16)
            for c in range(2):
                for j in range(4):
                    act.dma_start(abS[32 * j:32 * j + 32, c:c + 1],
                                  bass.AP(a_b.tensor, 512 * c + 128 * j, [[0, 8], [1, 4], [1, 1]])).then_inc(S("ws_in"), 16)
                    act.dma_start(wsS[32 * j:32 * j + 32, 4 * c:4 * c + 4],
                                  bass.AP(a_ws.tensor, (4 * c + j) * 128 * 128, [[0, 8], [128, 4], [1, 4]])).then_inc(S("ws_in"), 16)
            act.dma_start(abP[:, 0:8], a_b[0].rearrange("g t -> t g"), allow_slow_non_contiguous=True).then_inc(S("ws_in"), 16)
            steps = dict(index_weights=index_weights, index_prompt=index_prompt, index_sample=index_sample,
                         spatial_weights=spatial_weights, spatial=spatial)
            for n in range(N_OUT):
                evacuate(n)
                for what in AFTER[n]:
                    steps[what]() if isinstance(what, str) else item_layout(what[1])
                    if not isinstance(what, str) and what[1] in (3, 6):
                        store_item(what[1])
                if n == 7:
                    store_item(7)
                if n == 9:
                    store_item(8)
                if n == 0:
                    act.wait_ge(S("toep_out"), 16)
                    act.wait_ge(S("xnorm"), 3)
                    act.wait_ge(S("tr_ready"), 12)
                    act.dma_start(biasT, bass.AP(toep.tensor, 127, [[384, 128], [128 * 385, 8], [1, 256]])).then_inc(S("biasT_in"), 16)
                    store_item(0)

            def unit_attention(base, units, dest):
                for u in range(len(units) + 4):
                    if u < len(units):
                        nk = units[u][2]
                        act.wait_ge(S("unit_max"), base + u + 1)
                        A(SQv[:, u % 4, 0:nk], SQv[:, u % 4, 0:nk], ACT.Exp, bias=st_neg[:, u % 4:u % 4 + 1],
                          accum_out=st_sum[:, u % 4:u % 4 + 1]).then_inc(S("unit_exp"), 1)
                    v = u - 3
                    if 0 <= v < len(units):
                        nk = units[v][2]
                        act.wait_ge(S("unit_pt"), base + v + 1)
                        if v >= 2:
                            act.wait_ge(S("unit_o"), base + v - 1)
                        A(PTU[:, v % 2, 0:nk // 128, :], PS[:, 2 + v % 2, 0:nk].rearrange("p (c k) -> p c k", k=128),
                          ACT.Copy).then_inc(S("unit_pt_free"), 1)
                    v = u - 4
                    if 0 <= v < len(units):
                        act.wait_ge(S("unit_o"), base + v + 1)
                        A(dest(v), PS[:, 4 + v % 2, 0:128], ACT.Copy).then_inc(S("unit_o_free"), 1)

            unit_attention(0, UNITS, lambda v: mixT[:, 8 + UNITS[v][1], UNITS[v][0] * 128:UNITS[v][0] * 128 + 128])
            for b in range(8):
                if b:
                    act.wait_ge(S("s_qk"), b)
                for c in range(2):
                    for half in range(2):
                        g = 4 * b + 2 * c + half
                        act.wait_ge(S("kt_ready"), g + 1)
                        keys = KtH[:, c, :].rearrange("p (x r) -> p r x", r=8)[:, 4 * half:4 * half + 4, :]
                        A(keys, PS[:, 6 + g % 2, :].rearrange("p (r x) -> p r x", r=4), ACT.Copy).then_inc(S("kt_free"), 1)
                if b == 5:
                    act.wait_ge(S("s_max"), 1)
                    A(PB[:, 0, :], PSF[:, 0:NKEY], ACT.Exp, bias=st_neg[:, 0:1], accum_out=st_sum[:, 0:1])\
                        .then_inc(S("s_exp"), 1)
            act.wait_ge(S("s_max"), 2)
            A(PB[:, 1, :], PSF[:, 1536:1536 + NKEY], ACT.Exp, bias=st_neg[:, 1:2], accum_out=st_sum[:, 1:2])\
                .then_inc(S("s_exp"), 1)
            g = 32
            for x in range(2):
                for part in range(3):
                    act.wait_ge(S("kt_ready"), g + 1)
                    if part < 2:
                        A(PTs[:, x, part * 512:part * 512 + 512], PS[:, 6 + g % 2, :], ACT.Copy).then_inc(S("kt_free"), 1)
                    else:
                        A(PTs[0:R, x, 1024:1152], PS[0:R, 6 + g % 2, 0:128], ACT.Copy).then_inc(S("kt_free"), 1)
                    g += 1
            for x in range(2):
                act.wait_ge(S("s_o"), 4 * (x + 1))
                A(SQ[:, 256 * x:256 * x + 256], PS[:, x, 0:256], ACT.Copy).then_inc(S("s_o_sb"), 1)
            for x in range(2):
                act.wait_ge(S("kt_ready"), g + 1)
                for c in range(2):
                    last = A(mixT[:, 8 + 4 * c:12 + 4 * c, T + 16 * x:T + 16 * x + 16].rearrange("p h (b q) -> p h b q", b=4),
                             PS[:, 6 + g % 2, 128 * c:128 * c + 128].rearrange("p (b h q) -> p h b q", b=4, h=8)[:, 4 * c:4 * c + 4],
                             ACT.Copy)
                last.then_inc(S("kt_free"), 1)
                g += 1
            act.wait_ge(S("sums_zero"), 1)
            chunk_squares(1)
            evacuate(N_MQ)

            def lay_mem_keys(b, g):
                for r in range(2):
                    act.wait_ge(S("kt_ready"), g + r + 1)
                    if b >= 5 and r == 0:
                        act.wait_ge(S("m_qk"), b - 4)
                    A(mem_keys(b)[:, :, r * 128:r * 128 + 128], PS[:, 6 + (g + r) % 2, :].rearrange("p (h x) -> p h x", h=4),
                      ACT.Copy).then_inc(S("kt_free"), 1)
            for b in range(4):
                lay_mem_keys(b, g)
                g += 2
            item_layout(N_MQ)
            rw = routeW.rearrange("p (k n) -> p k n", k=KT)
            act.wait_ge(S("routew_zero"), 1)
            act.dma_start(rw[:, :, 0:4], w_group[0].rearrange("(p k) n -> p k n", k=KT)).then_inc(S("routew_in"), 16)
            act.dma_start(rw[:, :, 4:20], w_router[0].rearrange("(p k) n -> p k n", k=KT)).then_inc(S("routew_in"), 16)
            act.dma_start(routeB[:, 0:4], bass.AP(b_group.tensor, 0, [[0, 128], [1, 4]])).then_inc(S("routew_in"), 16)
            act.dma_start(routeB[:, 4:20], bass.AP(b_router.tensor, 0, [[0, 128], [1, 16]])).then_inc(S("routew_in"), 16)
            unit_attention(len(UNITS), UNITS_M, lambda v: moT[:, UNITS_M[v][1], UNITS_M[v][0] * 128:UNITS_M[v][0] * 128 + 128])
            for b in range(4, 8):
                lay_mem_keys(b, g)
                g += 2
            act.wait_ge(S("m_max"), 1)
            A(PBm, PS[:, 0, 0:256], ACT.Exp, bias=st_neg[:, 0:1], accum_out=st_sum[:, 0:1]).then_inc(S("m_exp"), 1)
            act.wait_ge(S("kt_ready"), g + 1)
            A(PTm, PS[:, 6 + g % 2, 0:256].rearrange("p (r x) -> p r x", r=2), ACT.Copy).then_inc(S("kt_free"), 1)
            g += 1
            act.wait_ge(S("m_o"), 8)
            A(SQ[:, :].rearrange("p (z n) -> p z n", z=2), PS[:, 1:3, :], ACT.Copy).then_inc(S("m_o_sb"), 1)
            for z in range(2):
                act.wait_ge(S("kt_ready"), g + 1)
                for h in range(4):
                    last = A(moT[:, h, T:NT].rearrange("p (b z q) -> p b z q", b=4, z=2)[:, :, z, :],
                             PS[:, 6 + g % 2, 128 * h:128 * h + 128].rearrange("p (b z h q) -> p b z h q", b=4, z=2, h=4)[:, :, z, h, :],
                             ACT.Copy)
                last.then_inc(S("kt_free"), 1)
                g += 1
            chunk_squares(2)
            act.wait_ge(S("r_sums"), 1)
            A(logitT, PS[:, 6, 0:NT], ACT.Copy).then_inc(S("r_sums_sb"), 1)
            for i in range(2):
                act.wait_ge(S("r_shifted"), i + 1)
                A(RX[i], RX[i], ACT.Exp).then_inc(S("r_exp"), 1)

            def y_rows(base):
                return [(ysc[bass.ds(base, CAP), half * 1024:half * 1024 + 1024], half) for half in range(2)]
            with act.Fori(0, NEXP // 2) as i:
                for k in range(2):
                    e = i * 2 + k
                    act.wait_ge(S("moe_free"), i * 12 + (6 * k + 10))
                    A(sg[64:128, :], PS[0:64, 2, :], ACT.Silu).then_inc(S("silu"), 1)
                    act.wait_ge(S("ht_ready"), e + 1)
                    A(hT, PS[:, 3, 0:256].rearrange("p (f r) -> p f r", f=4), ACT.Copy).then_inc(S("ht_laid"), 1)
                    act.wait_ge(S("y_out_psum"), e + 2)
                    for half in range(2):
                        act.dma_start(ysc[bass.ds(i * (2 * CAP) + k * CAP, CAP), half * 1024:half * 1024 + 1024],
                                      ysb[64 * half:64 * half + 64, k, :]).then_inc(S(f"y_out{k}"), 16)
            act.wait_ge(S("route_ready"), 1)
            nov = act.value_load(ids_nov, min_val=0, max_val=NOVF)
            with act.Fori(0, NOVF) as b:
                with act.If(b < nov):
                    act.wait_ge(S("moe_free"), b * 6 + (NLOT + 10))
                    A(sg[64:128, :], PS[0:64, 2, :], ACT.Silu).then_inc(S("ov_silu"), 1)
                    act.wait_ge(S("ov_ht"), b + 1)
                    A(hT, PS[:, 3, 0:256].rearrange("p (f r) -> p f r", f=4), ACT.Copy).then_inc(S("ov_ht_laid"), 1)
                    act.wait_ge(S("ov_y_sb"), b + 2)
                    for half in range(2):
                        act.dma_start(ysc[bass.ds(b * CAP + NEXP * CAP, CAP), half * 1024:half * 1024 + 1024],
                                      ysb[64 * half:64 * half + 64, 0, :]).then_inc(S("ov_stored"), 16)
            for name, count in stored:
                act.wait_ge(S(name), count)

        @block.vector
        def _(dve):
            V = nc.vector
            own = Chain(dve, "dve_step")
            V.memset(small[:, 200:212], 0.0).then_inc(S("sums_zero"), 1)
            TT, TS, STT = V.tensor_tensor, V.tensor_scalar, V.scalar_tensor_tensor

            def rsqrt(y, x, total, scale, a):
                own(TS(x, total, scale, EPS, ALU.mult, ALU.add))
                own(TS(y.bitcast(I32), x.bitcast(I32), 1, None, ALU.logical_shift_right))
                own(TS(y.bitcast(I32), y.bitcast(I32), -1.0, float(0x5f3759df), ALU.mult, ALU.add))
                for _ in range(3):
                    own(TT(a, y, y, ALU.mult))
                    own(STT(a, a, -0.5, x, ALU.mult, ALU.mult))
                    own(STT(y, a, 1.5, y, ALU.add, ALU.mult))

            def norm_rows(stage):
                def norm(t):
                    n = ROWS[t]
                    if stage == 0:
                        dve.wait_ge(S("rowsq"), t + 1)
                        rsqrt(xrs[0:n, t:t + 1], rx[0:n, t:t + 1], xss[0:n, t:t + 1], 1.0 / D, rt[0:n, t:t + 1])
                    out = hx[0:n, t, :] if stage == 0 else normed_rows(stage, t)[0:n, :]
                    TS(out, hx[0:n, t, :], xrs[0:n, t:t + 1], None, ALU.mult).then_inc(S("xnorm"), 1)

                def lay(t):
                    for q in range(4):
                        dve.wait_ge(S("tr_ready"), 12 * stage + 4 * t + q + 1)
                        TT(nT[:, 4 * q:4 * q + 4, t * 128:t * 128 + ROWS[t]],
                           PS[:, q, :].rearrange("p (k t) -> p k t", k=4)[:, :, 0:ROWS[t]],
                           bc(gcol[:, 16 * stage + 4 * q:16 * stage + 4 * q + 4], 2, [128, 4, ROWS[t]]),
                           ALU.mult).then_inc(S("tr_free"), 1)
                if stage:
                    dve.wait_ge(S("rowsq"), SQUARES[stage])
                    own(V.tensor_reduce(xss, sq_sums, AXX, ALU.add))
                    rsqrt(xrs, rx, xss, 1.0 / D, rt)
                norm(0)
                norm(1)
                if stage == 0:
                    dve.wait_ge(S("gcol_in"), 48)
                    dve.wait_ge(S("rowsq"), 3)
                lay(0)
                norm(2)
                lay(1)
                lay(2)

            def group_norm(x, g, count, gain, out=None):
                sq = SQ[:, 0:count * 128].rearrange("p (g d) -> p g d", g=count)
                own(TT(sq, x, x, ALU.mult))
                own(V.tensor_reduce(gsum[:, 0:count], sq, AXX, ALU.add))
                rsqrt(grs[:, 0:count], gx[:, 0:count], gsum[:, 0:count], 1.0 / 128, gt[:, 0:count])
                own(TT(x, x, bc(grs[:, 0:count], 2, [128, count, 128]), ALU.mult))
                return TT(x if out is None else out, x, gain, ALU.mult)

            def groups(ap):
                return ap.rearrange("p t (g d) -> p t g d", d=128)

            def prompt_groups(n, ng):
                return nat[:, n % 2, :, 0:ng * 128]

            def norm_item(n):
                kind, c, _ = ITEMS[n]
                b = n % 2
                dve.wait_ge(S("evac"), min(n, N_OUT) + 1)
                row = natS[:, b * 128:b * 128 + 128]
                if kind == "in" and c in (4, 5) or kind == "mq":
                    gain = gh[:, 0:128] if kind == "in" else gh[:, 256:384]
                    x = nat[:, b, :, :].rearrange("p t (g d) -> p (t g) d", d=128)
                    own(group_norm(x, 0, 8, bc(gain, 1, [128, 8, 128])))
                    group_norm(row.unsqueeze(1), 0, 1, gain.unsqueeze(1)).then_inc(S("normed"), 1)
                elif kind == "mk":
                    x = nat[:, b, :, :].rearrange("p t (g d) -> p (t g) d", d=128)
                    group_norm(x, 0, 8, bc(gh[:, 384:512], 1, [128, 8, 128])).then_inc(S("normed"), 1)
                elif c == 6:
                    gain = gh[:, 128:256]
                    for t in range(2):
                        x = nat[:, b, t, 0:256].rearrange("p (g d) -> p g d", d=128)
                        own(group_norm(x, 0, 2, bc(gain, 1, [128, 2, 128])))
                    group_norm(row.unsqueeze(1), 0, 1, gain.unsqueeze(1)).then_inc(S("normed"), 1)
                elif c in (2, 3):
                    x = nat[:, b, :, :].rearrange("p t (g d) -> p (t g) d", d=128)
                    cc_ = c - 2
                    sq = SQ[:, :].rearrange("p (g d) -> p g d", g=8)
                    own(TT(sq, x, x, ALU.mult))
                    own(V.tensor_reduce(gsum[:, 0:8], sq, AXX, ALU.add))
                    rsqrt(grs[:, 0:8], gx[:, 0:8], gsum[:, 0:8], 1.0 / 128, gt[:, 0:8])
                    own(TT(x, x, bc(grs[:, 0:8], 2, [128, 8, 128]), ALU.mult))
                    own(TT(vn[:, :, cc_ * 512:cc_ * 512 + 512], nat[:, b, :, :],
                           bc(gav[:, cc_ * 512:cc_ * 512 + 512], 1, [128, 2, 512]), ALU.mult))
                    group_norm(row.unsqueeze(1), 0, 1, gavS[:, cc_ * 128:cc_ * 128 + 128].unsqueeze(1),
                               out=vnS[:, cc_:cc_ + 1, :]).then_inc(S("normed"), 1)
                else:
                    dve.wait_ge(S("misc_free"), groups_through("spatial"))
                    own(TT(nat[:, b, :, :], nat[:, b, :, :], vn[:, :, c * 512:c * 512 + 512], ALU.mult))
                    TT(row, row, vnS[:, c, :], ALU.mult).then_inc(S("normed"), 1)

            def top_rounds(work, best, rounds):
                for _ in range(rounds):
                    own(V.max(best, work))
                    own(V.match_replace(work, best, work, TAKEN))

            own(V.memset(QZ[:, :], 0.0))
            norm_rows(0)
            dve.wait_ge(S("pt_in"), 16)
            pages = SQ[:, 0:64].rearrange("p (b j) -> p b j", b=8)
            own(TT(pages, ids[:, 16:80].rearrange("p (b j) -> p b j", b=8), bc(cc("page"), 1, [128, 8, 8]), ALU.mult))
            own(V.tensor_reduce(gsum[:, 0:8], pages, AXX, ALU.add))
            TS(gidx, gsum[:, 0:8], 16.0, cc("sub"), ALU.mult, ALU.add).then_inc(S("gidx_ready"), 1)
            dve.wait_ge(S("rel_in"), 16)
            TT(relX.rearrange("p (h q) -> p h q", h=8), bc(relR, 2, [128, 8, 4]),
               cc("relmask").rearrange("p (h q) -> p h q", h=8), ALU.mult).then_inc(S("rel_ready"), 1)
            dve.wait_ge(S("gh_in"), 16 * 9)
            own(TS(gh[:, 0:128], gh[:, 0:128], SCALE, None, ALU.mult))
            own(TS(gh[:, 256:384], gh[:, 256:384], SCALE, None, ALU.mult))
            dve.wait_ge(S("ws_in"), 16 * 17)
            for c in range(2):
                last = TT(SBLKn[:, c * 128:c * 128 + 128].rearrange("p (x t) -> p x t", t=4),
                          bc(wsS[:, 4 * c:4 * c + 4], 1, [128, 32, 4]), cc("blk").rearrange("p (x t) -> p x t", t=4), ALU.mult)
            last.then_inc(S("sblk_ready"), 1)
            dve.wait_ge(S("misc_free"), groups_through("index_weights"))
            TT(Wz[0:64, :].rearrange("p (b r) -> p b r", b=8), bc(wiM, 1, [64, 8, 32]),
               cc("wmask", 64).rearrange("p (b r) -> p b r", b=8), ALU.mult).then_inc(S("wz_ready"), 1)
            own(V.tensor_copy(workP[:, 0, 0:128], cc("causal")))
            own(V.memset(workP[:, 1, 0:128], 0.0))
            own(V.tensor_copy(workP[:, 1, 128:256], cc("causal")))
            for u in range(16):
                t, nk = u // 8, 128 * (u // 8 + 1)
                dve.wait_ge(S("misc_free"), groups_through("index_weights") + u + 1)
                for hh in range(2):
                    h = 4 * (u % 8 // 2) + 2 * hh + u % 2
                    last = STT(workP[:, t, 0:nk], RELU[:, u % 2, hh * 256:hh * 256 + nk], wiP[:, t * 16 + h:t * 16 + h + 1],
                               workP[:, t, 0:nk], ALU.mult, ALU.add)
                    if hh == 0:
                        own(last)
                last.then_inc(S("idxp_free"), 1)
                dve.wait_ge(S("idxp_free"), u + 1)
            best = top8[:, 0:8]
            bestS = top8[0:R, 8:16]
            for t in range(2):
                nk = 128 * (t + 1)
                top_rounds(workP[:, t, 0:nk], best, TOPK_P // 8)
                own(TS(workP[:, t, 0:nk], workP[:, t, 0:nk], TAKEN, -BIG, ALU.not_equal, ALU.mult))
                own(TT(workP[:, t, nk - 128:nk], workP[:, t, nk - 128:nk], cc("causal"), ALU.add))
            dve.wait_ge(S("idx_sum"), 8)
            own(V.tensor_copy(workS[0:R, 0:PAST], PSF[0:R, 1536:1536 + PAST]))
            TT(workS[0:R, PAST:NKEY], PSF[0:R, 1536 + PAST:1536 + NKEY], cc("newcausal", R), ALU.add).then_inc(S("scoreS"), 1)
            dve.wait_ge(S("scoreS"), 1)
            rounds = TOPK_S // 8

            def some_rounds(k):
                nonlocal rounds
                k = min(k, rounds)
                top_rounds(workS[0:R, :], bestS, k)
                rounds -= k
            for n in range(3, N_OUT):
                if ITEMS[n][0] != "mv":
                    norm_item(n)
                if n == 8:
                    dve.wait_ge(S("wsn_in"), 16)
                    TT(wsN, wsN, bc(cc("tril"), 1, [128, 8, 128]), ALU.mult).then_inc(S("ws_masked"), 1)
                some_rounds(TOPK_STEP)
            some_rounds(rounds)
            own(TS(workS[0:R, :], workS[0:R, :], TAKEN, -BIG, ALU.not_equal, ALU.mult))
            TT(workS[0:R, PAST:NKEY], workS[0:R, PAST:NKEY], cc("newcausal", R), ALU.add).then_inc(S("topkS"), 1)

            def unit_attention(base, units, masks):
                for u in range(len(units) + 1):
                    if u < len(units):
                        nk = units[u][2]
                        dve.wait_ge(S("unit_s"), base + u + 1)
                        if u >= 4:
                            dve.wait_ge(S("unit_pt"), base + u - 3)
                        buf, m = SQv[:, u % 4, 0:nk], masks(u)
                        if m:
                            TT(buf, PS[:, u % 2, 0:nk], m[0], ALU.add).then_inc(S("unit_added"), 1)
                            dve.wait_ge(S("unit_added"), base + u + 1)
                            own(TT(buf, buf, m[1], ALU.add))
                        else:
                            V.tensor_copy(buf, PS[:, u % 2, 0:nk]).then_inc(S("unit_added"), 1)
                            dve.wait_ge(S("unit_added"), base + u + 1)
                        V.tensor_reduce(st_neg[:, u % 4:u % 4 + 1], buf, AXX, ALU.max, negate=True).then_inc(S("unit_max"), 1)
                    v = u - 1
                    if v >= 0:
                        nk = units[v][2]
                        dve.wait_ge(S("unit_exp"), base + v + 1)
                        own(V.reciprocal(st_inv[:, v % 4:v % 4 + 1], st_sum[:, v % 4:v % 4 + 1]))
                        TS(SQv[:, v % 4, 0:nk], SQv[:, v % 4, 0:nk], st_inv[:, v % 4:v % 4 + 1], None, ALU.mult)\
                            .then_inc(S("unit_normed"), 1)
            dve.wait_ge(S("biasT_in"), 16)

            def own_masks(u):
                t, h, nk = UNITS[u]
                return biasT[:, h, 256 - nk:256], workP[:, t, 0:nk]
            unit_attention(0, UNITS, own_masks)

            def sample_softmax(x):
                dve.wait_ge(S("s_logits"), x + 1)
                V.tensor_reduce(st_neg[:, x:x + 1], PSF[:, 1536 * x:1536 * x + NKEY], AXX, ALU.max, negate=True).then_inc(S("s_max"), 1)
                dve.wait_ge(S("s_exp"), x + 1)
                own(V.reciprocal(st_inv[:, x:x + 1], st_sum[:, x:x + 1]))
                own(TS(PB[:, x, :], PB[:, x, :], st_inv[:, x:x + 1], None, ALU.mult))
                TT(PN[:, x * 32:x * 32 + 32].rearrange("p (b s) -> p b s", b=8), bc(PB[:, x, PAST:NKEY], 1, [128, 8, 4]),
                   cc("newmask")[:, x * 32:x * 32 + 32].rearrange("p (b s) -> p b s", b=8), ALU.mult).then_inc(S("s_probs"), 1)
            sample_softmax(0)
            sample_softmax(1)

            def add_chunk(c, n, total):
                dve.wait_ge(S("ring_free"), total)
                ps = 3 * (n % 2)
                cols = slice(512 * c, 512 * c + 512)
                TT(hx[:, 0:2, cols], hx[:, 0:2, cols], PS[:, ps:ps + 2, :], ALU.add)
                for j in range(4):
                    at = slice(512 * c + 128 * j, 512 * c + 128 * j + 128)
                    last = TT(hx[0:R, 2, at], hx[0:R, 2, at], PS[32 * j:32 * j + 32, ps + 2, 0:128], ALU.add)
                last.then_inc(S("h_add"), 1)
            dve.wait_ge(S("h_in"), 48)
            for c in range(4):
                add_chunk(c, N_OUT + c, 4 * (N_OUT + c + 1))
            own(V.memset(MQZ, 0.0))
            norm_rows(1)
            norm_item(N_MQ)
            V.memset(routeW, 0.0).then_inc(S("routew_zero"), 1)
            unit_attention(len(UNITS), UNITS_M, lambda u: None)
            dve.wait_ge(S("m_qk"), 8)
            V.tensor_reduce(st_neg[:, 0:1], PS[:, 0, 0:256], AXX, ALU.max, negate=True).then_inc(S("m_max"), 1)
            dve.wait_ge(S("m_exp"), 1)
            own(V.reciprocal(st_inv[:, 0:1], st_sum[:, 0:1]))
            TS(PBm, PBm, st_inv[:, 0:1], None, ALU.mult).then_inc(S("m_probs"), 1)
            for c in range(4):
                add_chunk(c, N_MQ + 1 + c, h_count + c + 1)
            norm_rows(2)

            dve.wait_ge(S("routew_in"), 64)
            dve.wait_ge(S("r_ready"), 1)
            own(V.memset(route, 0.0))
            own(TT(LG[:, 0:2, :], PS[:, 4, 0:40].rearrange("p (t n) -> p t n", t=2), bc(routeB, 1, [128, 2, 20]), ALU.add))
            own(TT(LG[0:R, 2, :], PS[0:R, 4, 40:60], routeB[0:R, :], ALU.add))
            m3 = r_max.unsqueeze(2).broadcast_to([128, 3, 4])
            desc = bc(r_desc, 1, [128, 3, 4])
            own(TS(r_desc, cc("iota_e")[:, 0:4], -1.0, 4.0, ALU.mult, ALU.add))

            def softmax(i, x):
                own(V.tensor_reduce(r_max, x, AXX, ALU.max))
                TT(RX[i], x, m3, ALU.subtract).then_inc(S("r_shifted"), 1)
                dve.wait_ge(S("r_exp"), i + 1)
                own(V.tensor_reduce(r_sum, RX[i], AXX, ALU.add))
                own(V.reciprocal(r_sum, r_sum))
                own(TT(RX[i], RX[i], bc(r_sum, 2, [128, 3, 4]), ALU.mult))

            def first_largest(out, x, largest):
                own(V.tensor_reduce(largest, x, AXX, ALU.max))
                own(TT(out, x, bc(largest, 2, [128, 3, 4]), ALU.is_ge))
                own(TT(out, out, desc, ALU.mult))
                own(V.tensor_reduce(r_sum, out, AXX, ALU.max))
                own(TT(out, out, bc(r_sum, 2, [128, 3, 4]), ALU.is_equal))
            softmax(0, LG[:, :, 0:4])
            first_largest(g_hot, RX[0], g_gate)
            for t in range(3):
                own(TT(AP3[:, t, :].rearrange("p (e g) -> p e g", e=4), LG[:, t, 4:20].rearrange("p (g e) -> p e g", g=4),
                       bc(g_hot[:, t, :], 1, [128, 4, 4]), ALU.mult))
            own(V.tensor_reduce(RX[1], AP3.rearrange("p t (e g) -> p t e g", e=4), AXX, ALU.add))
            softmax(1, RX[1])
            first_largest(e_hot[0], RX[1], e_val[0])
            own(STT(RX[1], e_hot[0], -2.0, RX[1], ALU.mult, ALU.add))
            first_largest(e_hot[1], RX[1], e_val[1])
            own(TT(r_sum, e_val[0], e_val[1], ALU.add))
            own(V.reciprocal(r_sum, r_sum))
            own(TT(r_sum, r_sum, g_gate, ALU.mult))
            for i in range(2):
                own(TT(w_tok[i], e_val[i], r_sum, ALU.mult))
                for t in range(3):
                    own(TT(AA[i][:, t, :].rearrange("p (g e) -> p g e", g=4), bc(g_hot[:, t, :], 2, [128, 4, 4]),
                           bc(e_hot[i][:, t, :], 1, [128, 4, 4]), ALU.mult))
            TT(AS, AA[0], AA[1], ALU.add).then_inc(S("picked"), 1)
            dve.wait_ge(S("rank_ready"), 1)
            own(V.tensor_copy(rank[:, 0:2, :], PS[:, 5, 0:32].rearrange("p (t e) -> p t e", t=2)))
            own(V.tensor_copy(rank[0:R, 2, :], PS[0:R, 5, 32:48]))
            count = PS[:, 5, 48:64]
            own(TS(extra, count, float(CAP), None, ALU.is_gt))
            for m in range(2, -(-NT // CAP)):
                own(STT(extra, count, float(m * CAP), extra, ALU.is_gt, ALU.add))
            own(V.tensor_copy(before[0], extra))
            at = 0
            for step in (1, 2, 4, 8):
                own(V.tensor_copy(before[1 - at][:, 0:step], before[at][:, 0:step]))
                own(TT(before[1 - at][:, step:16], before[at][:, step:16], before[at][:, 0:16 - step], ALU.add))
                at = 1 - at
            upto, under = before[at], before[1 - at]
            own(TT(under, upto, extra, ALU.subtract))
            own(TS(first_row, cc("iota_e"), float(CAP), None, ALU.mult))
            own(TS(over_row, under, float(CAP), float((NEXP - 1) * CAP), ALU.mult, ALU.add))
            for i in range(2):
                for table, out in ((rank, r_rank), (bc(first_row, 1, [128, 3, 16]), r_first),
                                   (bc(over_row, 1, [128, 3, 16]), r_over)):
                    own(TT(AP3, AA[i], table, ALU.mult))
                    own(V.tensor_reduce(out, AP3, AXX, ALU.add))
                own(TT(r_first, r_first, r_over, ALU.subtract))
                own(TS(r_sum, r_rank, float(CAP), None, ALU.is_lt))
                own(TT(r_first, r_first, r_sum, ALU.mult))
                own(TT(r_rank, r_rank, r_over, ALU.add))
                own(TT(ids[:, 80 + 3 * i:83 + 3 * i], r_rank, r_first, ALU.add))
            own(TS(ids_blk, ids_slot, 6, None, ALU.logical_shift_right))
            own(V.tensor_copy(r_blk, ids_blk))
            own(V.tensor_copy(r_row, ids_slot))
            own(STT(r_row, r_blk, -float(CAP), r_row, ALU.mult, ALU.add))
            own(TT(row_hot, bc(cc("iota_r"), 1, [128, 6, CAP]), bc(r_row, 2, [128, 6, CAP]), ALU.is_equal))
            own(TT(blk_tok, bc(cc("iota_r")[:, 0:NBLK], 1, [128, 6, NBLK]), bc(r_blk, 2, [128, 6, NBLK]), ALU.is_equal))
            for i in range(2):
                last = TT(blk_tok[:, 3 * i:3 * i + 3, :], blk_tok[:, 3 * i:3 * i + 3, :], bc(cc("tok"), 2, [128, 3, NBLK]), ALU.mult)
            last.then_inc(S("hot_ready"), 1)
            own(V.tensor_copy(ids_nov, upto[0:1, 15:16]))
            lo, hi = (ob.rearrange("p (b e) -> p b e", b=8) for ob in (own_lo, own_hi))
            own(TT(lo, bc(under[0:1, :], 1, [1, 8, 16]), bc(cc("iota_b", 1), 2, [1, 8, 16]), ALU.is_le))
            own(TT(hi, bc(upto[0:1, :], 1, [1, 8, 16]), bc(cc("iota_b", 1), 2, [1, 8, 16]), ALU.is_gt))
            own(TT(lo, lo, hi, ALU.mult))
            own(TT(lo, lo, bc(cc("iota_e", 1), 1, [1, 8, 16]), ALU.mult))
            own(V.tensor_reduce(r_own, lo, AXX, ALU.add))
            V.tensor_copy(ids_exp, r_own).then_inc(S("route_ready"), 1)
            dve.wait_ge(S("tab_sum"), 1)
            V.tensor_copy(tabS[0:CAP, :], PS[0:CAP, 7, 0:NBLK]).then_inc(S("tab_ready"), 1)

            def lay_rows():
                return TT(XT, PSF[:, 0:1024].rearrange("p (k r) -> p k r", k=KT), bc(gcol[:, 32:48], 2, [128, KT, CAP]), ALU.mult)
            dve.wait_ge(S("xt_ready"), 1)
            lay_rows().then_inc(S("xt_laid"), 1)
            with dve.Fori(0, NEXP // 2) as i:
                for k in range(2):
                    e = i * 2 + k
                    dve.wait_ge(S("silu"), e + 1)
                    TT(hid[64:128, :], sg[64:128, :], PS[64:128, 2, :], ALU.mult).then_inc(S("hidden"), 1)
                    dve.wait_ge(S("xt_ready"), e + 2)
                    lay_rows().then_inc(S("xt_laid"), 1)
                    dve.wait_ge(S("moe_free"), i * 12 + (6 * k + 12))
                    dve.wait_ge(S(f"y_out{k}"), i * 32 + 32)
                    V.tensor_copy(ysb[:, k, :], PSF[:, 2048:3072]).then_inc(S("y_out_psum"), 1)
            nov = dve.value_load(ids_nov, min_val=0, max_val=NOVF)
            dve.wait_ge(S("y_out0"), 32 * (NEXP // 2 + 1))
            with dve.Fori(0, NOVF) as b:
                with dve.If(b < nov):
                    dve.wait_ge(S("ov_silu"), b + 1)
                    TT(hid[64:128, :], sg[64:128, :], PS[64:128, 2, :], ALU.mult).then_inc(S("ov_hidden"), 1)
                    dve.wait_ge(S("xt_ready"), b + (NEXP + 2))
                    lay_rows().then_inc(S("xt_laid"), 1)
                    dve.wait_ge(S("moe_free"), b * 6 + (NLOT + 12))
                    dve.wait_ge(S("ov_stored"), b * 32 + 32)
                    V.tensor_copy(ysb[:, 0, :], PSF[:, 2048:3072]).then_inc(S("ov_y_sb"), 1)
            for t in range(3):
                n = ROWS[t]
                g0, g1 = G[2 * t][0:n, :], G[2 * t + 1][0:n, :]
                dve.wait_ge(S(f"g_in{t}"), 32)
                own(TS(g0, g0, w_tok[0][0:n, t:t + 1], None, ALU.mult))
                own(STT(g0, g1, w_tok[1][0:n, t:t + 1], g0, ALU.mult, ALU.add))
                TT(hx[0:n, t, :], hx[0:n, t, :], g0, ALU.add).then_inc(S("y_ready"), 1)


_INS = ['x_prompt', 'x_sample', 'cache_k', 'cache_v', 'cache_idx_k', 'cache_mem_k', 'cache_mem_v', 'page_table',
        'mem_prompt', 'norm_mix', 'w_in', 'a_vnorm', 'a_ws', 'a_b', 'b_qnorm', 'b_knorm', 'rel_bias', 'w_out',
        'norm_mem', 'mem_wq', 'mem_wk', 'mem_wv', 'mem_qnorm', 'mem_knorm', 'mem_wo', 'norm_ffn', 'w_group',
        'b_group', 'w_router', 'b_router', 'w_gate', 'w_up', 'w_down']
_OUTS = [(1, T, D), (NB, NS, D), (1, 1, T, 2, 128), (1, 1, T, 2, 128), (1, 1, T, 64), (1, 1, 256, 4, 128),
         (1, 1, 256, 4, 128), (1, NB, NS, 2, 128), (1, NB, NS, 2, 128), (1, NB, NS, 64), (1, NB, NS, 8, 128)]


def kernel(**inputs):
    import numpy as _np
    import concourse.bacc as _bacc
    from concourse import mybir as _mybir
    from concourse.bass_utils import run_bass_kernel_spmd as _run

    nc = _bacc.Bacc("TRN2", target_bir_lowering=False, num_devices=1)
    consts, buckets = shape_constants()
    arrays = {"in_consts": consts, "in_buckets": buckets}
    for name in _INS:
        arrays[f"in_{name}"] = _np.ascontiguousarray(inputs[name])
    args = [nc.dram_tensor(n, a.shape, _mybir.dt.from_np(a.dtype), kind="ExternalInput").ap()
            for n, a in arrays.items()]
    for i, shape in enumerate(_OUTS):
        args.append(nc.dram_tensor(f"out_{i}", shape, F32, kind="ExternalOutput").ap())
    decode_step(nc, *args)
    r = _run(nc, [arrays], core_ids=[0])
    return tuple(r.results[0][f"out_{i}"] for i in range(len(_OUTS)))
```
